# Optimizing a Trainium2 kernel written in Bass

```python
import jax, jax.numpy as jnp
from jax import lax
import numpy as np

D_MODEL = 1024
BATCH = 1
SEQ = 256
DEPTH = 2

CHUNK = 64
Q_BLOCK = 128
EPS = 1e-6
HEAD_DIM = 64
FOX_HEADS = 8
FOX_W = FOX_HEADS * HEAD_DIM
SB_HEADS = 8
SB_W = SB_HEADS * HEAD_DIM
MLA_HEADS = 8
MLA_Q_RANK = 384
MLA_KV_RANK = 256
MLA_NOPE = 64
MLA_ROPE = 32
MLA_V = 64
MLA_W = MLA_HEADS * MLA_V
ROPE_BASE = 10000.0
N_BRANCH = 3
D_FF = -(-8 * D_MODEL // (3 * 256)) * 256

SPLIT_WIDTHS = (3 * FOX_W, FOX_HEADS, MLA_Q_RANK, MLA_KV_RANK, MLA_ROPE, 3 * SB_W, N_BRANCH * D_MODEL)
IN_WIDTH = int(sum(SPLIT_WIDTHS))
SPLIT_POINTS = [int(p) for p in np.cumsum(SPLIT_WIDTHS)[:-1]]


def rms_norm(x, g):
    xf = x.astype(jnp.float32)
    y = xf * lax.rsqrt(jnp.mean(xf * xf, axis=-1, keepdims=True) + EPS)
    return (y * g.astype(jnp.float32)).astype(x.dtype)

def rope_tables(positions, dim):
    half = dim // 2
    inv = ROPE_BASE ** (-jnp.arange(half, dtype=jnp.float32) / half)
    ang = positions.astype(jnp.float32)[..., None] * inv
    return jnp.cos(ang), jnp.sin(ang)

def apply_rope(x, cos, sin):
    x1, x2 = jnp.split(x.astype(jnp.float32), 2, axis=-1)
    out = jnp.concatenate([x1 * cos - x2 * sin, x1 * sin + x2 * cos], axis=-1)
    return out.astype(x.dtype)

def to_heads(t, n_heads):
    b, s, w = t.shape
    return t.reshape(b, s, n_heads, w // n_heads).transpose(0, 2, 1, 3)

def merge_heads(t):
    b, h, s, d = t.shape
    return t.transpose(0, 2, 1, 3).reshape(b, s, h * d)

def to_blocks(t):
    b, h, s = t.shape[:3]
    t = t.reshape((b, h, s // Q_BLOCK, Q_BLOCK) + t.shape[3:])
    return jnp.moveaxis(t, 2, 0)

def from_blocks(t):
    nb, b, h, qb = t.shape[:4]
    return jnp.moveaxis(t, 0, 2).reshape((b, h, nb * qb) + t.shape[4:])

def fox_attention(q, k, v, log_f):
    s = q.shape[2]
    scale = q.shape[-1] ** -0.5
    cum = jnp.cumsum(log_f, axis=-1)
    kpos = jnp.arange(s)
    starts = jnp.arange(s // Q_BLOCK) * Q_BLOCK

    def block(args):
        qb, fq, start = args
        qpos = start + jnp.arange(Q_BLOCK)
        logits = jnp.einsum('bhqd,bhkd->bhqk', qb, k, preferred_element_type=jnp.float32) * scale
        logits = logits + fq[..., None] - cum[..., None, :]
        logits = jnp.where(kpos[None, :] <= qpos[:, None], logits, -jnp.inf)
        p = jax.nn.softmax(logits, axis=-1)
        return jnp.einsum('bhqk,bhkd->bhqd', p.astype(v.dtype), v)

    return from_blocks(lax.map(block, (to_blocks(q), to_blocks(cum), starts)))

def mla_attention(q_nope, q_rope, k_nope, k_rope, v):
    s = q_nope.shape[2]
    scale = (MLA_NOPE + MLA_ROPE) ** -0.5
    kchunk = jnp.arange(s) // CHUNK
    starts = jnp.arange(s // Q_BLOCK) * Q_BLOCK

    def block(args):
        qn, qr, start = args
        qchunk = (start + jnp.arange(Q_BLOCK)) // CHUNK
        logits = (jnp.einsum('bhqn,bhkn->bhqk', qn, k_nope, preferred_element_type=jnp.float32)
                  + jnp.einsum('bhqr,bkr->bhqk', qr, k_rope, preferred_element_type=jnp.float32)) * scale
        logits = jnp.where(kchunk[None, :] <= qchunk[:, None], logits, -jnp.inf)
        p = jax.nn.softmax(logits, axis=-1)
        return jnp.einsum('bhqk,bhkv->bhqv', p.astype(v.dtype), v)

    return from_blocks(lax.map(block, (to_blocks(q_nope), to_blocks(q_rope), starts)))

def stick_breaking_attention(q, k, v):
    s = q.shape[2]
    scale = q.shape[-1] ** -0.5
    kpos = jnp.arange(s)
    starts = jnp.arange(s // Q_BLOCK) * Q_BLOCK

    def block(args):
        qb, start = args
        qpos = start + jnp.arange(Q_BLOCK)
        mask = kpos[None, :] < qpos[:, None]
        z = jnp.einsum('bhqd,bhkd->bhqk', qb, k, preferred_element_type=jnp.float32) * scale
        log_beta = jax.nn.log_sigmoid(z)
        log_keep = jnp.where(mask, jax.nn.log_sigmoid(-z), 0.0)
        suffix = lax.cumsum(log_keep, axis=3, reverse=True) - log_keep
        a = jnp.where(mask, jnp.exp(log_beta + suffix), 0.0)
        return jnp.einsum('bhqk,bhkd->bhqd', a.astype(v.dtype), v)

    return from_blocks(lax.map(block, (to_blocks(q), starts)))

def first_inputs(seed: int = 0) -> dict:
    key = jax.random.key(seed)
    ks = jax.random.split(key, 24)

    def nrm(k, shape, fan_in, gain=1.0):
        return jax.random.normal(k, shape, jnp.float32) * (gain * fan_in ** -0.5)

    def gain(k, shape):
        return 1.0 + 0.1 * jax.random.normal(k, shape, jnp.float32)

    x = jax.random.normal(ks[0], (BATCH, SEQ, D_MODEL), jnp.float32)
    c = jax.random.normal(ks[1], (BATCH, D_MODEL), jnp.float32)
    offs = jax.random.randint(ks[2], (BATCH, 1), 0, 10000, dtype=jnp.int32)
    positions = jnp.arange(SEQ, dtype=jnp.int32)[None, :] + offs
    return {
        "x": x,
        "c": c,
        "positions": positions,
        "g_mix": gain(ks[3], (DEPTH, D_MODEL)),
        "w_ada": nrm(ks[4], (DEPTH, D_MODEL, 6 * D_MODEL), D_MODEL, 0.5),
        "b_ada": 0.01 * jax.random.normal(ks[5], (DEPTH, 6 * D_MODEL), jnp.float32),
        "w_in": nrm(ks[6], (DEPTH, D_MODEL, IN_WIDTH), D_MODEL),
        "b_fox_f": jax.random.uniform(ks[7], (DEPTH, FOX_HEADS), jnp.float32, 1.0, 5.0),
        "g_mla_q": gain(ks[8], (DEPTH, MLA_Q_RANK)),
        "w_mla_uq": nrm(ks[9], (DEPTH, MLA_Q_RANK, MLA_HEADS * (MLA_NOPE + MLA_ROPE)), MLA_Q_RANK),
        "g_mla_kv": gain(ks[10], (DEPTH, MLA_KV_RANK)),
        "w_mla_ukv": nrm(ks[11], (DEPTH, MLA_KV_RANK, MLA_HEADS * (MLA_NOPE + MLA_V)), MLA_KV_RANK),
        "w_o_fox": nrm(ks[12], (DEPTH, FOX_W, D_MODEL), FOX_W),
        "w_o_mla": nrm(ks[13], (DEPTH, MLA_W, D_MODEL), MLA_W),
        "w_o_sb": nrm(ks[14], (DEPTH, SB_W, D_MODEL), SB_W),
        "w_out": nrm(ks[15], (DEPTH, D_MODEL, D_MODEL), D_MODEL),
        "g_ffn": gain(ks[16], (DEPTH, D_MODEL)),
        "w_ffn_gate": nrm(ks[17], (DEPTH, D_MODEL, D_FF), D_MODEL),
        "w_ffn_up": nrm(ks[18], (DEPTH, D_MODEL, D_FF), D_MODEL),
        "w_ffn_down": nrm(ks[19], (DEPTH, D_FF, D_MODEL), D_FF),
        "g_final": gain(ks[20], (D_MODEL,)),
    }

def first_block(x, c, positions, g_mix, w_ada, b_ada, w_in, b_fox_f, g_mla_q, w_mla_uq, g_mla_kv,
              w_mla_ukv, w_o_fox, w_o_mla, w_o_sb, w_out, g_ffn, w_ffn_gate, w_ffn_up, w_ffn_down,
              g_final):
    b, s, d = x.shape
    cos, sin = rope_tables(positions, MLA_ROPE)
    cond = jax.nn.silu(c)
    for l in range(DEPTH):
        mod = (cond @ w_ada[l] + b_ada[l]).reshape(b, 6, d)
        sh_a, sc_a, gt_a, sh_f, sc_f, gt_f = [mod[:, i, None, :] for i in range(6)]

        u = rms_norm(x, g_mix[l]) * (1 + sc_a) + sh_a
        proj = u @ w_in[l]
        fox_qkv, fox_f, mla_ql, mla_kvl, mla_kr, sb_qkv, gate_logit = jnp.split(proj, SPLIT_POINTS, axis=-1)

        fq, fk, fv = [to_heads(t, FOX_HEADS) for t in jnp.split(fox_qkv, 3, axis=-1)]
        log_f = jax.nn.log_sigmoid((fox_f + b_fox_f[l]).astype(jnp.float32)).transpose(0, 2, 1)
        y_fox = merge_heads(fox_attention(fq, fk, fv, log_f))

        cq = rms_norm(mla_ql, g_mla_q[l])
        q = to_heads(cq @ w_mla_uq[l], MLA_HEADS)
        q_nope = q[..., :MLA_NOPE]
        q_rope = apply_rope(q[..., MLA_NOPE:], cos[:, None], sin[:, None])
        ckv = rms_norm(mla_kvl, g_mla_kv[l])
        kv = to_heads(ckv @ w_mla_ukv[l], MLA_HEADS)
        k_nope, mla_v = kv[..., :MLA_NOPE], kv[..., MLA_NOPE:]
        k_rope = apply_rope(mla_kr, cos, sin)
        y_mla = merge_heads(mla_attention(q_nope, q_rope, k_nope, k_rope, mla_v))

        sq, sk, sv = [to_heads(t, SB_HEADS) for t in jnp.split(sb_qkv, 3, axis=-1)]
        y_sb = merge_heads(stick_breaking_attention(sq, sk, sv))

        g = jax.nn.sigmoid(gate_logit.astype(jnp.float32)).astype(x.dtype).reshape(b, s, N_BRANCH, d)
        merged = (g[:, :, 0] * (y_fox @ w_o_fox[l])
                  + g[:, :, 1] * (y_mla @ w_o_mla[l])
                  + g[:, :, 2] * (y_sb @ w_o_sb[l]))
        x = x + gt_a * (merged @ w_out[l])

        u = rms_norm(x, g_ffn[l]) * (1 + sc_f) + sh_f
        h = jax.nn.silu(u @ w_ffn_gate[l]) * (u @ w_ffn_up[l])
        x = x + gt_f * (h @ w_ffn_down[l])
    return rms_norm(x, g_final)


GRID_W = 64
CTX_LEN = 256
NEG_INF = -1e30

NA_HEADS = 8
NA_HEAD_DIM = 64
NA_WIDTH = NA_HEADS * NA_HEAD_DIM
NA_KH = 8
NA_KW = 16
SGU_GROUPS = 8
SGU_WIDTH = D_MODEL - NA_WIDTH
SGU_GROUP_DIM = SGU_WIDTH // SGU_GROUPS
SGU_CHUNK = 128
HYB_IN = 3 * NA_WIDTH + 2 * SGU_WIDTH

RET_HEADS = 8
RET_QK_DIM = D_MODEL // RET_HEADS
RET_V_DIM = 2 * RET_QK_DIM
RET_QK_WIDTH = RET_HEADS * RET_QK_DIM
RET_V_WIDTH = RET_HEADS * RET_V_DIM
RET_CHUNK = 128
RET_IN = 2 * RET_QK_WIDTH + 2 * RET_V_WIDTH

D_FF_2 = 2816
CONV_W = 3

N_EVEN = (DEPTH + 1) // 2
N_ODD = DEPTH // 2


def rmsnorm(x, g):
    xf = x.astype(jnp.float32)
    y = xf * lax.rsqrt(jnp.mean(xf * xf, axis=-1, keepdims=True) + EPS)
    return (y * g.astype(jnp.float32)).astype(x.dtype)

def modulate(x, shift, scale):
    return x * (1 + scale) + shift

def axial_rope(n_tokens, head_dim):
    t = jnp.arange(n_tokens)
    row = (t // GRID_W).astype(jnp.float32)
    col = (t % GRID_W).astype(jnp.float32)
    n_freq = head_dim // 4
    inv = ROPE_BASE ** (-jnp.arange(n_freq, dtype=jnp.float32) / n_freq)
    ang = jnp.concatenate([row[:, None] * inv, col[:, None] * inv], axis=-1)
    return jnp.cos(ang), jnp.sin(ang)

def apply_rope_2(x, cos, sin):
    x1, x2 = jnp.split(x, 2, axis=-1)
    c = cos[None, :, None, :]
    s = sin[None, :, None, :]
    return jnp.concatenate([x1 * c - x2 * s, x1 * s + x2 * c], axis=-1).astype(x.dtype)

def neighbourhood_attention(q, k, v, k_ctx, v_ctx, rpb):
    B, T, H, dh = q.shape
    rows = T // GRID_W
    kh = min(NA_KH, rows)
    kw = NA_KW
    scale = dh ** -0.5
    qg = q.reshape(B, rows, GRID_W, H, dh)
    kg = k.reshape(B, rows, GRID_W, H, dh)
    vg = v.reshape(B, rows, GRID_W, H, dh)
    r = jnp.arange(rows)
    r0 = jnp.clip(r - kh // 2, 0, rows - kh)
    key_rows = r0[:, None] + jnp.arange(kh)[None, :]
    k_blk = kg[:, key_rows].reshape(B, rows, kh * GRID_W, H, dh)
    v_blk = vg[:, key_rows].reshape(B, rows, kh * GRID_W, H, dh)
    s_nb = jnp.einsum('brqhd,brkhd->bhrqk', qg, k_blk,
                      preferred_element_type=jnp.float32) * scale
    cidx = jnp.arange(GRID_W)
    c0 = jnp.clip(cidx - kw // 2, 0, GRID_W - kw)
    in_win = (cidx[None, :] >= c0[:, None]) & (cidx[None, :] < c0[:, None] + kw)
    mask = jnp.broadcast_to(in_win[:, None, :], (GRID_W, kh, GRID_W)).reshape(GRID_W, kh * GRID_W)
    dr = key_rows - r[:, None] + (NA_KH - 1)
    dc = jnp.clip(cidx[None, :] - cidx[:, None], -(kw - 1), kw - 1) + (kw - 1)
    bias = rpb[:, dr[:, None, :, None], dc[None, :, None, :]]
    bias = bias.reshape(H, rows, GRID_W, kh * GRID_W).astype(jnp.float32)
    s_nb = jnp.where(mask, s_nb + bias[None], NEG_INF)
    s_cx = jnp.einsum('brqhd,bchd->bhrqc', qg, k_ctx,
                      preferred_element_type=jnp.float32) * scale
    p = jax.nn.softmax(jnp.concatenate([s_nb, s_cx], axis=-1), axis=-1)
    n_nb = kh * GRID_W
    p_nb = p[..., :n_nb].astype(v.dtype)
    p_cx = p[..., n_nb:].astype(v.dtype)
    o = (jnp.einsum('bhrqk,brkhd->brqhd', p_nb, v_blk)
         + jnp.einsum('bhrqc,bchd->brqhd', p_cx, v_ctx))
    return o.reshape(B, T, H * dh).astype(q.dtype)

def context_attention(q, k, v):
    B, L, H, dh = q.shape
    s = jnp.einsum('bqhd,bkhd->bhqk', q, k, preferred_element_type=jnp.float32) * dh ** -0.5
    p = jax.nn.softmax(s, axis=-1).astype(v.dtype)
    return jnp.einsum('bhqk,bkhd->bqhd', p, v).reshape(B, L, H * dh).astype(q.dtype)

def spatial_gating(u, v, w_s, b_s):
    B, N, _ = v.shape
    vf = v.astype(jnp.float32)
    mu = jnp.mean(vf, axis=-1, keepdims=True)
    var = jnp.mean(jnp.square(vf - mu), axis=-1, keepdims=True)
    vn = ((vf - mu) * lax.rsqrt(var + EPS)).astype(v.dtype)
    vc = vn.reshape(B, N // SGU_CHUNK, SGU_CHUNK, SGU_GROUPS, SGU_GROUP_DIM)
    mixed = jnp.einsum('gpq,bnqgc->bnpgc', w_s, vc) + b_s.T[None, None, :, :, None]
    return u * mixed.reshape(B, N, SGU_WIDTH)

def hybrid_na_sgu(h_ctx, h_lat, w_in, rpb, w_s, b_s, w_out, ctx_out):
    heads = lambda a: a.reshape(a.shape[0], a.shape[1], NA_HEADS, NA_HEAD_DIM)
    splits = [NA_WIDTH, 2 * NA_WIDTH, 3 * NA_WIDTH, 3 * NA_WIDTH + SGU_WIDTH]
    q, k, v, u, g = jnp.split(h_lat @ w_in, splits, axis=-1)
    if ctx_out:
        qc, kc, vc, uc, gc = jnp.split(h_ctx @ w_in, splits, axis=-1)
    else:
        kc, vc = jnp.split(h_ctx @ w_in[:, NA_WIDTH:3 * NA_WIDTH], 2, axis=-1)
    a_lat = neighbourhood_attention(heads(q), heads(k), heads(v), heads(kc), heads(vc), rpb)
    s_lat = spatial_gating(jax.nn.gelu(u), jax.nn.gelu(g), w_s, b_s)
    y_lat = jnp.concatenate([a_lat, s_lat], axis=-1) @ w_out
    y_ctx = None
    if ctx_out:
        a_ctx = context_attention(heads(qc), heads(kc), heads(vc))
        s_ctx = spatial_gating(jax.nn.gelu(uc), jax.nn.gelu(gc), w_s, b_s)
        y_ctx = jnp.concatenate([a_ctx, s_ctx], axis=-1) @ w_out
    return y_ctx, y_lat

def retention_chunked(q, k, v, lg, state0):
    B, N, H, dk = q.shape
    dv = v.shape[-1]
    C = RET_CHUNK
    n = N // C
    to_chunks = lambda a: a.reshape(B, n, C, H, a.shape[-1]).transpose(1, 0, 3, 2, 4)
    pos = jnp.arange(C, dtype=jnp.float32)
    diff = pos[:, None] - pos[None, :]
    lower = diff >= 0
    decay_intra = jnp.where(lower[None], jnp.exp(lg[:, None, None] * jnp.where(lower, diff, 0.0)[None]), 0.0)
    decay_q = jnp.exp(lg[:, None] * (pos + 1.0))[None, :, :, None]
    decay_k = jnp.exp(lg[:, None] * (C - 1.0 - pos))[None, :, :, None]
    decay_chunk = jnp.exp(lg * C)[None, :, None, None]

    def step(S, blk):
        qb, kb, vb = blk
        qf = qb.astype(jnp.float32)
        kf = kb.astype(jnp.float32)
        vf = vb.astype(jnp.float32)
        s = jnp.einsum('bhqd,bhkd->bhqk', qf, kf) * decay_intra
        o = jnp.einsum('bhqk,bhkv->bhqv', s, vf) + jnp.einsum('bhqd,bhdv->bhqv', qf * decay_q, S)
        S = S * decay_chunk + jnp.einsum('bhkd,bhkv->bhdv', kf * decay_k, vf)
        return S, o

    _, o = lax.scan(step, state0, (to_chunks(q), to_chunks(k), to_chunks(v)))
    return o.transpose(1, 0, 3, 2, 4).reshape(B, N, H, dv)

def retention_final_state(k, v, lg):
    L = k.shape[1]
    w = jnp.exp(lg[None, :] * (L - 1.0 - jnp.arange(L, dtype=jnp.float32))[:, None])
    return jnp.einsum('blhd,blhv->bhdv', k.astype(jnp.float32) * w[None, :, :, None], v.astype(jnp.float32))

def retention_output(o, g, gn_g, w_out):
    B, N = o.shape[0], o.shape[1]
    mu = jnp.mean(o, axis=-1, keepdims=True)
    var = jnp.mean(jnp.square(o - mu), axis=-1, keepdims=True)
    on = ((o - mu) * lax.rsqrt(var + EPS)).reshape(B, N, RET_V_WIDTH) * gn_g.astype(jnp.float32)
    return (jax.nn.silu(g) * on.astype(g.dtype)) @ w_out

def retention_mixer(h_ctx, h_lat, w_in, log_decay, gn_g, w_out, ctx_out):
    B, T, _ = h_lat.shape
    L = h_ctx.shape[1]
    H, dk, dv = RET_HEADS, RET_QK_DIM, RET_V_DIM
    splits = [RET_QK_WIDTH, 2 * RET_QK_WIDTH, 2 * RET_QK_WIDTH + RET_V_WIDTH]
    q, k, v, g = jnp.split(h_lat @ w_in, splits, axis=-1)
    cos, sin = axial_rope(T, dk)
    q = apply_rope_2(q.reshape(B, T, H, dk), cos, sin)
    k = apply_rope_2(k.reshape(B, T, H, dk) * dk ** -0.5, cos, sin)
    v = v.reshape(B, T, H, dv)
    if ctx_out:
        qc, kc, vc, gc = jnp.split(h_ctx @ w_in, splits, axis=-1)
        qc = qc.reshape(B, L, H, dk)
    else:
        kc, vc = jnp.split(h_ctx @ w_in[:, RET_QK_WIDTH:2 * RET_QK_WIDTH + RET_V_WIDTH], [RET_QK_WIDTH], axis=-1)
    kc = kc.reshape(B, L, H, dk) * dk ** -0.5
    vc = vc.reshape(B, L, H, dv)
    outs_lat = []
    outs_ctx = []
    for d in range(2):
        lg = log_decay[d].astype(jnp.float32)
        rev = (lambda a: a[:, ::-1]) if d == 1 else (lambda a: a)
        s_ctx = retention_final_state(rev(kc), rev(vc), lg)
        outs_lat.append(rev(retention_chunked(rev(q), rev(k), rev(v), lg, s_ctx)))
        if ctx_out:
            outs_ctx.append(rev(retention_chunked(rev(qc), rev(kc), rev(vc), lg, jnp.zeros_like(s_ctx))))
    y_lat = retention_output(outs_lat[0] + outs_lat[1], g, gn_g, w_out)
    y_ctx = None
    if ctx_out:
        y_ctx = retention_output(outs_ctx[0] + outs_ctx[1], gc, gn_g, w_out)
    return y_ctx, y_lat

def dwconv3(x, w, b):
    xp = jnp.pad(x, ((0, 0), (1, 1), (0, 0)))
    return xp[:, :-2] * w[0] + xp[:, 1:-1] * w[1] + xp[:, 2:] * w[2] + b

def conv_ffn(h, w_in, conv_w, conv_b, w_out):
    a = dwconv3(h @ w_in, conv_w, conv_b)
    gate, up = jnp.split(a, 2, axis=-1)
    return (jax.nn.silu(gate) * up) @ w_out

def second_inputs(seed: int = 0) -> dict:
    key = jax.random.key(seed)
    ks = jax.random.split(key, 20)
    nrm = lambda k, shape, s: jax.random.normal(k, shape, jnp.float32) * s
    base_decay = np.log1p(-2.0 ** (-5.0 - np.arange(RET_HEADS))).astype(np.float32)
    return {
        "x": nrm(ks[0], (BATCH, SEQ, D_MODEL), 1.0),
        "c": nrm(ks[1], (BATCH, D_MODEL), 1.0),
        "ctx": nrm(ks[2], (BATCH, CTX_LEN, D_MODEL), 1.0),
        "c_ctx": nrm(ks[3], (D_MODEL,), 1.0),
        "ada_w": nrm(ks[4], (DEPTH, D_MODEL, 6 * D_MODEL), 0.5 * D_MODEL ** -0.5),
        "ada_b": nrm(ks[5], (DEPTH, 6 * D_MODEL), 0.02),
        "norm_g": 1.0 + nrm(ks[6], (DEPTH, 4, D_MODEL), 0.1),
        "hyb_w_in": nrm(ks[7], (N_EVEN, D_MODEL, HYB_IN), D_MODEL ** -0.5),
        "na_rpb": nrm(ks[8], (N_EVEN, NA_HEADS, 2 * NA_KH - 1, 2 * NA_KW - 1), 0.1),
        "sgu_w": nrm(ks[9], (N_EVEN, SGU_GROUPS, SGU_CHUNK, SGU_CHUNK), SGU_CHUNK ** -0.5),
        "sgu_b": 1.0 + nrm(ks[10], (N_EVEN, SGU_GROUPS, SGU_CHUNK), 0.1),
        "hyb_w_out": nrm(ks[11], (N_EVEN, D_MODEL, D_MODEL), D_MODEL ** -0.5),
        "ret_w_in": nrm(ks[12], (N_ODD, D_MODEL, RET_IN), D_MODEL ** -0.5),
        "ret_log_decay": jnp.asarray(base_decay)[None, None, :] * (1.0 + nrm(ks[13], (N_ODD, 2, RET_HEADS), 0.05)),
        "ret_gn_g": 1.0 + nrm(ks[14], (N_ODD, RET_V_WIDTH), 0.1),
        "ret_w_out": nrm(ks[15], (N_ODD, RET_V_WIDTH, D_MODEL), RET_V_WIDTH ** -0.5),
        "ffn_w_in": nrm(ks[16], (DEPTH, D_MODEL, 2 * D_FF_2), D_MODEL ** -0.5),
        "ffn_conv_w": nrm(ks[17], (DEPTH, CONV_W, 2 * D_FF_2), CONV_W ** -0.5),
        "ffn_conv_b": nrm(ks[18], (DEPTH, 2 * D_FF_2), 0.02),
        "ffn_w_out": nrm(ks[19], (DEPTH, D_FF_2, D_MODEL), D_FF_2 ** -0.5),
    }

def second_block(x, c, ctx, c_ctx, ada_w, ada_b, norm_g, hyb_w_in, na_rpb, sgu_w, sgu_b, hyb_w_out,
              ret_w_in, ret_log_decay, ret_gn_g, ret_w_out, ffn_w_in, ffn_conv_w, ffn_conv_b, ffn_w_out):
    xc = ctx
    silu_c = jax.nn.silu(c)
    silu_cc = jax.nn.silu(c_ctx)
    for i in range(DEPTH):
        ctx_out = i < DEPTH - 1
        j = i // 2
        mod_lat = (silu_c @ ada_w[i] + ada_b[i])[:, None, :]
        mod_ctx = (silu_cc @ ada_w[i] + ada_b[i])[None, None, :]
        sh1, sc1, g1, sh2, sc2, g2 = jnp.split(mod_lat, 6, axis=-1)
        csh1, csc1, cg1, csh2, csc2, cg2 = jnp.split(mod_ctx, 6, axis=-1)
        h_lat = modulate(rmsnorm(x, norm_g[i, 0]), sh1, sc1)
        h_ctx = modulate(rmsnorm(xc, norm_g[i, 0]), csh1, csc1)
        if i % 2 == 0:
            y_ctx, y_lat = hybrid_na_sgu(h_ctx, h_lat, hyb_w_in[j], na_rpb[j], sgu_w[j], sgu_b[j],
                                         hyb_w_out[j], ctx_out)
        else:
            y_ctx, y_lat = retention_mixer(h_ctx, h_lat, ret_w_in[j], ret_log_decay[j], ret_gn_g[j],
                                           ret_w_out[j], ctx_out)
        x = x + g1 * rmsnorm(y_lat, norm_g[i, 1])
        h = modulate(rmsnorm(x, norm_g[i, 2]), sh2, sc2)
        x = x + g2 * rmsnorm(conv_ffn(h, ffn_w_in[i], ffn_conv_w[i], ffn_conv_b[i], ffn_w_out[i]), norm_g[i, 3])
        if ctx_out:
            xc = xc + cg1 * rmsnorm(y_ctx, norm_g[i, 1])
            hc = modulate(rmsnorm(xc, norm_g[i, 2]), csh2, csc2)
            xc = xc + cg2 * rmsnorm(conv_ffn(hc, ffn_w_in[i], ffn_conv_w[i], ffn_conv_b[i], ffn_w_out[i]), norm_g[i, 3])
    return x


def setup_inputs(seed=0):
    out = dict(first_inputs(seed))
    for name, value in second_inputs(seed + 1).items():
        if name != "x":
            out[name + "_2"] = value
    return out


def reference(
    x, c, positions, g_mix, w_ada, b_ada, w_in, b_fox_f, g_mla_q, w_mla_uq, g_mla_kv, w_mla_ukv,
    w_o_fox, w_o_mla, w_o_sb, w_out, g_ffn, w_ffn_gate, w_ffn_up, w_ffn_down, g_final, c_2,
    ctx_2, c_ctx_2, ada_w_2, ada_b_2, norm_g_2, hyb_w_in_2, na_rpb_2, sgu_w_2, sgu_b_2,
    hyb_w_out_2, ret_w_in_2, ret_log_decay_2, ret_gn_g_2, ret_w_out_2, ffn_w_in_2, ffn_conv_w_2,
    ffn_conv_b_2, ffn_w_out_2,
):
    x = first_block(
        x, c, positions, g_mix, w_ada, b_ada, w_in, b_fox_f, g_mla_q, w_mla_uq, g_mla_kv,
        w_mla_ukv, w_o_fox, w_o_mla, w_o_sb, w_out, g_ffn, w_ffn_gate, w_ffn_up, w_ffn_down,
        g_final,
    )
    return second_block(
        x, c_2, ctx_2, c_ctx_2, ada_w_2, ada_b_2, norm_g_2, hyb_w_in_2, na_rpb_2, sgu_w_2,
        sgu_b_2, hyb_w_out_2, ret_w_in_2, ret_log_decay_2, ret_gn_g_2, ret_w_out_2, ffn_w_in_2,
        ffn_conv_w_2, ffn_conv_b_2, ffn_w_out_2,
    )


_drawn_inputs = setup_inputs


def setup_inputs(seed=0):
    import zlib

    import numpy as np

    out = dict(_drawn_inputs(seed))
    spreads = {}
    factors = {'b_ada': 3.357,
     'g_mla_q': 8.0,
     'g_mla_kv': 4.997,
     'na_rpb_2': 27.712,
     'ffn_conv_b_2': 5.203,
     'sgu_b_2': 2.843}
    for name, (base, spread) in spreads.items():
        noise = np.random.default_rng([zlib.crc32(name.encode()), seed]).standard_normal(out[name].shape)
        drawn = base * np.exp(spread * noise) if base else spread * noise
        out[name] = __import__('jax').numpy.asarray(drawn.astype(out[name].dtype))
    for name, factor in factors.items():
        out[name] = (out[name] * factor).astype(out[name].dtype)
    return out
```

```python
from contextlib import ExitStack

import numpy as np

import concourse.bass as bass
from concourse import mybir

F32 = mybir.dt.float32
I32 = mybir.dt.int32
ACT = mybir.ActivationFunctionType
ALU = mybir.AluOpType
AX = mybir.AxisListType

P = 128
T = 256
D = 1024
KD = D // P
DEPTH = 2
H = 8
DH = 64
W = H * DH
WT = W // P
MLA_Q, MLA_KV, ROPE = 384, 256, 32
KQ, KKV = MLA_Q // P, MLA_KV // P
DFF = 2816
FT = DFF // P
EPS = 1e-6
NEG = -1e30
N_ADA = 6 * KD
N_COND = 3

TILE = P
TILES_PER_PANEL = 16
PANEL = TILES_PER_PANEL * TILE
RING = 7
BANKS = 7
ADA_BANK = 7
STEPS = 3 * H

ADA_PANELS = N_ADA * KD // TILES_PER_PANEL
TILES_1 = (KD + 3 * 4 * KD + KQ * KD + KKV * KD + 2 * KD + 3 * 4 * KD + (4 + 2 + 2) * KQ + 8 * KKV
           + 3 * KD * KD + 3 * KD * WT + KD * KD + N_ADA * KD + 2 * FT * KD + KD * FT)
PANELS_1 = -(-TILES_1 // TILES_PER_PANEL)
assert PANELS_1 % RING == 0

PAR1 = {}
for _name, _n in (("b_ada", N_ADA), ("g_mix", KD), ("g_ffn", KD), ("g_q", KQ), ("g_kv", KKV), ("b_fox", 1)):
    PAR1[_name] = (sum(n for _, n in PAR1.values()), _n)
N_PAR1 = sum(n for _, n in PAR1.values())


T2 = 2 * T
CONV = 3
GRID, WIN = 64, 16
ROWS = T // GRID
RPB_H, RPB_W = 15, 31
RV = 256
RVT = H * RV // P
PAR2 = {}
for _name, _n in (("b_ada", N_ADA), ("norm_g", 4 * KD), ("conv_w", CONV * 2 * FT), ("conv_b", 2 * FT)):
    PAR2[_name] = (sum(n for _, n in PAR2.values()), _n)
N_PAR2 = sum(n for _, n in PAR2.values())
MISC = {}
for _name, _n in (("g_final", KD), ("gn_g", RVT), ("log_decay", 2 * H)):
    MISC[_name] = (sum(n for _, n in MISC.values()), _n)
N_MISC = sum(n for _, n in MISC.values())
TILES_2 = ((3 * 4 + 8) * KD + KD * KD + 2 * FT * KD + KD * FT + N_ADA * KD,
           (2 * KD + RVT) * KD + RVT * KD + KD * RVT + 2 * FT * KD + KD * FT)
PANELS_2 = [-(-t // TILES_PER_PANEL) for t in TILES_2]


def shape_constants():
    p = np.arange(P)[:, None]
    j = np.arange(P)[None, :]
    c = {}
    c["ident"] = (p == j) * 1.0
    c["mean_d"] = np.full((P, P), 1.0 / D)
    c["mean_q"] = np.full((P, P), 1.0 / MLA_Q)
    c["mean_kv"] = np.full((P, P), 1.0 / MLA_KV)
    c["ones"] = np.ones((P, P))
    c["eps"] = np.full((P, 1), EPS)
    causal = np.where(j <= p, 0.0, NEG)
    chunk = np.where(j // 64 <= p // 64, 0.0, NEG)
    zero = np.zeros((P, P))
    c["mask_fox"] = np.concatenate([causal, zero, causal], 1)
    c["mask_mla"] = np.concatenate([chunk, zero, chunk], 1)
    c["before"] = (p < j) * 1.0
    c["after"] = (p > j) * 1.0
    first = np.clip(p % GRID - WIN // 2, 0, GRID - WIN)
    k = np.arange(GRID)[None, :]
    c["na_mask"] = np.where((k >= first) & (k < first + WIN), 0.0, NEG)
    inv = (10000.0 ** (-np.arange(ROPE // 2, dtype=np.float64) / (ROPE // 2))).astype(np.float32)
    c["inv_freq"] = inv[np.arange(P) % (ROPE // 2)][:, None]
    c["rope_sign"] = np.where(p % ROPE < ROPE // 2, -1.0, 1.0)
    return {k: np.ascontiguousarray(v, dtype=np.float32) for k, v in c.items()}


def retention_constants():
    key = np.arange(T2).reshape(4, P).T[:, :, None]
    q = np.arange(T)[None, None, :]
    ahead = np.where(key < T, q - key, q - key + T2)
    behind = np.where(key < T, key - q, key - q)
    dist = np.stack([np.maximum(ahead, 0), np.maximum(behind, 0)], 1).reshape(P, 8, T)
    mask = np.stack([ahead >= 0, behind >= 0], 1)[:, :, 0:2, :].reshape(P, 4, T)
    return dist.astype(np.float32), mask.astype(np.float32)


def axial_rope():
    n = P // 4
    t = np.arange(T)
    inv = (10000.0 ** (-np.arange(n, dtype=np.float64) / n)).astype(np.float32)
    ang = np.concatenate([(t // GRID).astype(np.float32)[:, None] * inv, (t % GRID).astype(np.float32)[:, None] * inv], 1)
    cos, sin = np.cos(ang.astype(np.float64)).T, np.sin(ang.astype(np.float64)).T
    return np.stack([np.concatenate([cos, cos]), np.concatenate([sin, -sin])], 1).astype(np.float32)


def columns(arrays):
    at, out = 0, {}
    for k, v in arrays.items():
        out[k] = (at, v.shape[1])
        at += v.shape[1]
    return out, at


def stationary(w):
    k, f = w.shape
    return w.reshape(k // P, P, f // P, P).transpose(2, 0, 1, 3).reshape(-1, P, P)


def streaming(w):
    k, f = w.shape
    return w.reshape(k // P, P, f // 512, 4, P).transpose(2, 0, 3, 1, 4).reshape(-1, P, P)


def panels(tiles):
    t = np.concatenate(tiles)
    pad = -len(t) % TILES_PER_PANEL
    if pad:
        t = np.concatenate([t, np.zeros((pad, P, P), np.float32)])
    return t.reshape(-1, TILES_PER_PANEL, P, P).transpose(0, 2, 1, 3).reshape(-1, P, PANEL)


def tape_block1(i, l, ada_next):
    w = i["w_in"][l]
    fox, mq, mkv = 3 * W, MLA_Q, MLA_KV
    at = np.cumsum([0, fox, H, mq, mkv, ROPE, 3 * W, 3 * D])
    sec = [w[:, a:b] for a, b in zip(at[:-1], at[1:])]
    out = []
    f_pad = np.zeros((D, P), np.float32)
    f_pad[:, :H] = sec[1]
    out += [stationary(f_pad), stationary(sec[0][:, :2 * W]), streaming(sec[0][:, 2 * W:])]
    out += [stationary(sec[2]), stationary(sec[3])]
    kr = sec[4]
    swap = np.concatenate([np.arange(ROPE // 2, ROPE), np.arange(ROPE // 2)])
    out += [stationary(np.tile(kr, (1, 4))), stationary(np.tile(kr[:, swap], (1, 4)))]
    out += [stationary(sec[5][:, :2 * W]), streaming(sec[5][:, 2 * W:])]
    uq = i["w_mla_uq"][l].reshape(MLA_Q, H, DH + ROPE)
    rope = uq[:, :, DH:]
    out += [stationary(uq[:, :, :DH].reshape(MLA_Q, W)), stationary(rope.reshape(MLA_Q, H * ROPE)),
            stationary(rope[:, :, swap].reshape(MLA_Q, H * ROPE))]
    ukv = i["w_mla_ukv"][l].reshape(MLA_KV, H, 2 * DH)
    out += [stationary(ukv[:, :, :DH].reshape(MLA_KV, W)), streaming(ukv[:, :, DH:].reshape(MLA_KV, W))]
    out += [stationary(sec[6])]
    out += [stationary(i[n][l]) for n in ("w_o_fox", "w_o_mla", "w_o_sb")]
    out += [stationary(i["w_out"][l])]
    ada = stationary(ada_next)
    out += [ada[:32]]
    g, u = stationary(i["w_ffn_gate"][l]), stationary(i["w_ffn_up"][l])
    for f in range(FT):
        out += [g[f * KD:f * KD + KD], u[f * KD:f * KD + KD], ada[32 + 16 * f:48 + 16 * f]]
    out += [stationary(i["w_ffn_down"][l])]
    return panels(out)


def tape_block2(i, j, ada_next):
    out = []
    if j == 0:
        q, k, v, su, sg = np.split(i["hyb_w_in_2"][0], 5, axis=1)
        out += [stationary(q), stationary(k), streaming(sg), stationary(su), streaming(v), stationary(i["hyb_w_out_2"][0])]
    else:
        w = i["ret_w_in_2"][0]
        q, k, v, g = np.split(w, [D, 2 * D, 2 * D + H * RV], axis=1)
        out += [stationary(q), stationary(k), streaming(v), stationary(g), stationary(i["ret_w_out_2"][0])]
    w = stationary(i["ffn_w_in_2"][j])
    ada = None if ada_next is None else stationary(ada_next)
    for f in range(FT):
        out += [w[f * KD:(f + 1) * KD], w[(FT + f) * KD:(FT + f + 1) * KD]]
        if ada is not None:
            n = 2 if f < FT - 2 else 4
            at = 2 * f if f < FT - 2 else 2 * (FT - 2) + 4 * (f - FT + 2)
            out += [ada[at * KD:(at + n) * KD]]
    out += [stationary(i["ffn_w_out_2"][j])]
    return panels(out)


def bias_window(rpb):
    t = np.arange(T)
    row, col = t // GRID, t % GRID
    dr = row[None, :] - row[:, None] + RPB_H // 2
    dc = np.clip(col[None, :] - col[:, None], -(WIN - 1), WIN - 1) + RPB_W // 2
    return np.ascontiguousarray(rpb[:, dr, dc].reshape(H, 2, P, T).transpose(2, 1, 0, 3))


def feature_major(v):
    return np.asarray(v).reshape(-1, P).T


class Signal:

    def __init__(self, sem, per_layer):
        self.sem, self.per_layer = sem, per_layer

    def __call__(self, n, layer=0):
        assert 0 <= n < self.per_layer
        return self.sem, layer * self.per_layer + n + 1


def order_block1():
    o = ["stat_mix", "fox_f"] + [f"fox_qk{f}" for f in range(2 * WT)] + ["fox_v0", "fox_v1"]
    o += [f"lat{f}" for f in range(KQ + KKV)] + ["k_rope", "k_swap"]
    o += [f"sb_qk{f}" for f in range(2 * WT)] + ["sb_v0", "sb_v1", "stat_q", "stat_kv"]
    o += [f"mla_q{f}" for f in range(WT)] + [f"q_{n}{f}" for n in ("rope", "swap") for f in range(2)]
    o += [f"mla_k{f}" for f in range(WT)] + ["mla_v0", "mla_v1"]
    for i in range(STEPS + 2):
        if i < STEPS:
            o += [f"score{i}", f"gate{i}"]
        if i >= STEPS:
            o += [f"branch{i - STEPS}_{f}" for f in range(KD)]
        if 1 <= i <= STEPS:
            o.append(f"keys{i - 1}")
        if i >= 2:
            o.append(f"pv{i - 2}")
    o += [f"branch2_{f}" for f in range(KD)] + [f"w_out{f}" for f in range(KD)] + ["stat_ffn"]
    for f in range(FT):
        o += [f"ffn_gate{f}", f"ffn_up{f}"]
    return o + [f"down{f}" for f in range(KD)]



def order_block2():
    def ffn(j):
        o = [f"norm{2 + 2 * j}"]
        o += [f"conv{j}_{f}_{n}" for f in range(FT) for n in range(2)]
        return o + [f"out{1 + 2 * j}_{f}" for f in range(KD)] + [f"post{1 + 2 * j}"]

    o = ["norm0", "norm1"] + [f"na_qk{f}" for f in range(2 * WT)] + [f"sgu_g{b}" for b in range(4)]
    o += [f"sgu_u{f}" for f in range(WT)] + [f"na_v{b}" for b in range(4)]
    for i in range(2 * H + 2):
        if i < 2 * H:
            o += [f"na_score{2 * i + q}" for q in range(2)] if i < H else [f"na_score{H + i}"]
        n = i - 1
        if 0 <= n < 2 * H:
            o += [f"na_keys{2 * n + q}" for q in range(2)] if n < H else [f"na_keys{H + n}"]
        if i >= 2:
            o.append(f"na_pv{i - 2}")
    o += [f"mix{t}" for t in range(WT)] + [f"out0_{f}" for f in range(KD)] + ["post0"] + ffn(0)
    o += ["norm3"] + [f"ret_qk{f}" for f in range(2 * H)] + [f"ret_v{c}_{b}" for c in range(4) for b in range(4)]
    o += [f"ret_g{f}" for f in range(RVT)]
    for i in range(H + 3):
        if i < H:
            o += [f"ret_score{i}_0", f"ret_score{i}_1"]
        if 0 <= i - 1 < H:
            o.append(f"ret_o{i - 1}")
        if 0 <= i - 2 < H:
            o.append(f"ret_mean{i - 2}")
        if 0 <= i - 3 < H:
            o.append(f"ret_var{i - 3}")
    return o + [f"out2_{f}" for f in range(KD)] + ["post2"] + ffn(1)


def two_blocks(nc, tape, consts, par1, cond_in, pos_in, x_in, par2_in, misc_in, ctx_in, bias_in, sgu_w_in, sgu_b_in, axial,
               dist_in, mask_in, out):
    n_panels = tape.shape[0]
    assert n_panels % RING == 0
    cat, n_const = columns(shape_constants())
    ORDER = order_block1()
    GROUP = {name: g for g, name in enumerate(ORDER)}

    with ExitStack() as ctx:
        def sb(name, *shape, dt=F32):
            return ctx.enter_context(nc.sbuf_tensor(name, [P, *shape], dt))

        def semaphore(name):
            return ctx.enter_context(nc.semaphore(name))

        def signal(name, per_layer):
            return Signal(semaphore(name), per_layer)

        ring = sb("ring", RING, PANEL)
        x = sb("x", KD, 2 * T)
        u = sb("u", KD, 2 * T)
        work = sb("work", 26950)
        cst = sb("cst", n_const)
        par1_all = sb("par1_all", DEPTH, N_PAR1)
        par = sb("par", N_PAR1)
        mod = sb("mod", N_ADA, N_COND)
        gs_mix = sb("gs_mix", KD)
        gs_ffn = sb("gs_ffn", KD)
        cond = sb("cond", KD, N_COND)
        cond_e = sb("cond_e", KD, N_COND)
        cond_r = sb("cond_r", KD, N_COND)
        rope_c = sb("rope_c", T)
        rope_s = sb("rope_s", T)
        ps = ctx.enter_context(nc.psum_tensor("ps", [P, 8, 512], F32))

        taken = [0]

        def carve(*shape):
            n = int(np.prod(shape))
            a = taken[0]
            taken[0] += n
            assert taken[0] <= 26950, taken[0]
            v = work[:, a:a + n]
            if len(shape) == 2:
                v = v.rearrange("p (a b) -> p a b", a=shape[0])
            if len(shape) == 3:
                v = v.rearrange("p (a b c) -> p a b c", a=shape[0], b=shape[1])
            return v

        def const(name):
            a, n = cat[name]
            return cst[:, a:a + n]

        def par_of(name):
            a, n = PAR1[name]
            return par[:, a:a + n]

        xt = x[:, :, 0:T]
        flat_u = u[:, :, :].rearrange("p k t -> p (k t)")
        u1 = flat_u[:, 0:KD * T].rearrange("p (k t) -> p k t", k=KD)
        sq = flat_u[:, KD * T:2 * KD * T].rearrange("p (k t) -> p k t", k=KD)
        merged = u1
        fox_qk, fox_v = carve(2 * WT, T), carve(2, W)
        sb_qk, sb_v = carve(2 * WT, T), carve(2, W)
        hidden = work[:, 0:FT * T].rearrange("p (f t) -> p f t", f=FT)
        assert taken[0] >= FT * T
        latent = carve(KQ + KKV, T)
        mla_q, mla_k, mla_v = carve(WT, T), carve(WT, T), carve(2, W)
        q_rope, k_rope = carve(2, T), carve(T)
        sigma = carve(STEPS, T)
        y = carve(3 * WT, T)
        start_steps = taken[0]
        probs = carve(3, 3 * P)
        keys = carve(2, 3 * P)
        soft, log_beta, log_keep = carve(3, 3 * P), carve(3, 3 * P), carve(3, 3 * P)
        end_steps = taken[0]
        taken[0] = start_steps
        ffn_e, ffn_gu, ffn_r = carve(3, T), carve(3, T), carve(3, T)
        taken[0] = end_steps
        gated = carve(2, T)
        rstds = [carve(T), keys[:, 0, 0:T], keys[:, 1, 0:T]]
        neg_max, sums, recips = carve(STEPS, 2), carve(STEPS, 2), carve(STEPS, 2)
        fox_t, fox_l = gated[:, 0, :], gated[:, 1, :]
        flat_soft = soft.rearrange("p a b -> p (a b)")
        rope_t = flat_soft[:, 0:2 * T].rearrange("p (a b) -> p a b", a=2)
        neg_cum = log_beta[:, 0, 0:T]

        taken[0] = 0
        na_qk = carve(2 * WT, T2)
        sgu_in = carve(2 * WT, T2)
        na_v = carve(4, W)
        sgu_w, sgu_b = carve(H, P), carve(WT, P)
        na_bias = carve(2, H, T)
        branches = carve(KD, T2)
        flat_probs = work[:, taken[0]:taken[0] + KD * T2]
        na_probs, na_keys = carve(3, 2, T2), carve(2, 4, T)
        end_first = taken[0]
        taken[0] = 0
        ret_q, ret_k = carve(H, T), carve(H, T2)
        ret_v = carve(4, H * RV)
        ret_g = carve(RVT, T)
        decay, decay_b = carve(2, 4, T), carve(4, T)
        decayed = carve(2, 4, T)
        ret_o = carve(3, 2, T)
        ret_mask = carve(4, T)
        taken[0] = max(taken[0], end_first)
        rstd2 = carve(T2)
        ln_sum, ln_var, ln_rstd = carve(4), carve(4), carve(4)
        na_max, na_sum, na_recip = carve(2 * H, 2), carve(2 * H, 2), carve(2 * H, 2)
        sgu_t = branches[:, WT:2 * WT, :].rearrange("p a b -> p (a b)").rearrange("p (a b) -> p a b", a=2)
        wide_sq = flat_probs[:, 0:KD * T2].rearrange("p (k t) -> p k t", k=KD)
        wide_y = na_bias.rearrange("p a b c -> p (a b c)").rearrange("p (k t) -> p k t", k=KD)
        wide_hidden = work[:, 0:FT * T2].rearrange("p (f t) -> p f t", f=FT)
        wide_conv = branches.rearrange("p a b -> p (a b)")[:, 0:6 * T2].rearrange("p (a b c) -> p a b c", a=3, b=2)
        assert FT * T2 <= 4 * 2 * WT * T2 // 2 + 4 * W + H * P
        ret_dist = x[:, :, T:T2]
        ret_t = decayed.rearrange("p a b c -> p (a b c)").rearrange("p (a b) -> p a b", a=8)
        ret_e = u[:, :, :].rearrange("p k t -> p (k t)").rearrange("p (f t) -> p f t", f=RVT)
        ret_rstd = rstd2.rearrange("p (a b) -> p a b", a=2)
        thin_y = ret_q
        thin_sq = ret_k[:, :, 0:T]
        thin_hidden = ret_v.rearrange("p a b -> p (a b)")[:, 0:FT * T].rearrange("p (f t) -> p f t", f=FT)
        thin_conv = ret_g.rearrange("p a b -> p (a b)")[:, 0:6 * T].rearrange("p (a b c) -> p a b c", a=3, b=2)

        par2 = sb("par2", DEPTH, N_PAR2)
        misc = sb("misc", N_MISC)
        gains = sb("gains", 4, 2, KD)

        def par2_of(j, name, a=0, n=None):
            at, width = PAR2[name]
            return par2[:, j, at + a:at + a + (width if n is None else n)]

        def misc_of(name):
            at, width = MISC[name]
            return misc[:, at:at + width]

        landed = [semaphore(f"panel_landed{s}") for s in range(RING)]
        panel_used = semaphore("panel_used")
        loaded = {n: semaphore(f"loaded_{n}") for n in ("cst", "par1", "cond", "pos", "x")}
        stored = semaphore("stored")
        prep_act = signal("prep_act", 3)
        prep = signal("prep", 17)
        ada_done = signal("ada_done", 1)
        group_done = signal("group_done", len(ORDER))
        mod_made = signal("mod_made", 4)
        squared = signal("squared", 2 * KD)
        log_mean = signal("log_mean", 4)
        rstd_made = signal("rstd_made", 4)
        scaled = signal("scaled", 2 * KD)
        u_made = signal("u_made", 2 * KD)
        fox_soft = signal("fox_soft", 3)
        fox_low = signal("fox_low", 1)
        cum_made = signal("cum_made", 1)
        qk_made = signal("qk_made", 4 * WT)
        v_made = signal("v_made", 6)
        lat_made = signal("lat_made", KQ + KKV)
        lat_sq = signal("lat_sq", KQ + KKV)
        lat_norm = signal("lat_norm", KQ + KKV)
        rope_mul = signal("rope_mul", 6)
        rope_made = signal("rope_made", 3)
        nope_made = signal("nope_made", 2 * WT)
        masked = signal("masked", 2 * H)
        max_made = signal("max_made", 4 * H)
        exp_made = signal("exp_made", 4 * H)
        recip_made = signal("recip_made", 2 * H)
        probs_made = signal("probs_made", 4 * H)
        keys_made = signal("keys_made", 2 * H)
        z_soft = signal("z_soft", 3 * H)
        beta_made = signal("beta_made", H)
        keep_made = signal("keep_made", H)
        keep_masked = signal("keep_masked", H)
        stick_log = signal("stick_log", H)
        stick_exp = signal("stick_exp", H)
        stick_made = signal("stick_made", H)
        gate_exp = signal("gate_exp", STEPS)
        gate_one = signal("gate_one", STEPS)
        sigma_made = signal("sigma_made", STEPS)
        y_made = signal("y_made", STEPS)
        gated_made = signal("gated_made", 3 * KD)
        merged_made = signal("merged_made", 2 * KD)
        x_mixed = signal("x_mixed", KD)
        ffn_exp = signal("ffn_exp", FT)
        ffn_prod = signal("ffn_prod", FT)
        ffn_one = signal("ffn_one", FT)
        ffn_recip = signal("ffn_recip", FT)
        hidden_made = signal("hidden_made", FT)
        x_done = signal("x_done", KD)

        FREED = {"stat_mix": (log_mean, 0), "fox_f": (fox_low, 0), "k_rope": (rope_mul, 0), "k_swap": (rope_mul, 1),
                 "stat_q": (log_mean, 1), "stat_kv": (log_mean, 2), "stat_ffn": (log_mean, 3)}
        for f in range(2 * WT):
            FREED[f"fox_qk{f}"], FREED[f"sb_qk{f}"] = (qk_made, f), (qk_made, 2 * WT + f)
        for n, branch in enumerate(("fox", "sb", "mla")):
            for b in range(2):
                FREED[f"{branch}_v{b}"] = (v_made, 2 * n + b)
        for f in range(KQ + KKV):
            FREED[f"lat{f}"] = (lat_sq, f)
        for f in range(2):
            FREED[f"q_rope{f}"], FREED[f"q_swap{f}"] = (rope_mul, 2 + 2 * f), (rope_mul, 3 + 2 * f)
        for f in range(WT):
            FREED[f"mla_q{f}"], FREED[f"mla_k{f}"] = (nope_made, f), (nope_made, WT + f)
        for s in range(STEPS):
            FREED[f"gate{s}"], FREED[f"pv{s}"] = (gate_exp, s), (y_made, s)
            FREED[f"score{s}"] = (masked, s) if s < 2 * H else (keep_made, s - 2 * H)
            FREED[f"keys{s}"] = (keys_made, s) if s < 2 * H else (stick_log, s - 2 * H)
        for f in range(KD):
            for b in range(3):
                FREED[f"branch{b}_{f}"] = (gated_made, b * KD + f)
            FREED[f"w_out{f}"], FREED[f"down{f}"] = (x_mixed, f), (x_done, f)
        for f in range(FT):
            FREED[f"ffn_gate{f}"], FREED[f"ffn_up{f}"] = (ffn_prod, f), (hidden_made, f)

        def bank(name):
            return ps[:, GROUP[name] % BANKS]

        def done(name, l):
            return group_done(GROUP[name], l)

        NORMS, POSTS = 5, 4
        ROOT = {name: n for n, name in enumerate(("norm0", "norm1", "post0", "norm2", "post1", "norm3", "post2", "norm4", "post3"))}
        for n in ("par2", "misc", "ctx", "na", "axial", "dist", "mask"):
            loaded[n] = semaphore(f"loaded_{n}")
        ORDER2 = order_block2()
        GROUP2 = {name: g for g, name in enumerate(ORDER2)}
        group2_done = signal("group2_done", len(ORDER2))
        squared2 = signal("squared2", NORMS * KD)
        log_mean2 = signal("log_mean2", NORMS + POSTS)
        rstd2_made = signal("rstd2_made", NORMS + POSTS)
        scaled2 = signal("scaled2", NORMS * KD)
        u2_made = signal("u2_made", (NORMS - 1) * KD)
        mod2_made = signal("mod2_made", 2 * 9)
        y2_copied = signal("y2_copied", POSTS * KD)
        y2_squared = signal("y2_squared", POSTS * KD)
        y2_scaled = signal("y2_scaled", POSTS * KD)
        x2_made = signal("x2_made", POSTS * KD)
        conv_mid = signal("conv_mid", 4 * FT)
        conv_left = signal("conv_left", 4 * FT)
        conv_made = signal("conv_made", 4 * FT)
        conv_exp = signal("conv_exp", 2 * FT)
        conv_one = signal("conv_one", 2 * FT)
        conv_recip = signal("conv_recip", 2 * FT)
        conv_silu = signal("conv_silu", 2 * FT)
        hidden2_made = signal("hidden2_made", 2 * FT)
        na_qk_made = signal("na_qk_made", 2 * WT)
        sgu_copied = signal("sgu_copied", 2 * WT)
        na_v_made = signal("na_v_made", 4)
        gelu_sq = signal("gelu_sq", 4)
        gelu_poly = signal("gelu_poly", 8)
        gelu_in = signal("gelu_in", 4)
        gelu_exp = signal("gelu_exp", 4)
        gelu_one = signal("gelu_one", 4)
        gelu_recip = signal("gelu_recip", 4)
        gelu_made = signal("gelu_made", 4)
        ln_steps = signal("ln_steps", 6)
        ln_sq = signal("ln_sq", 4)
        ln_root = signal("ln_root", 2)
        ln_made = signal("ln_made", 4)
        bias_masked = signal("bias_masked", 2)
        NA_PARTS = 3 * H
        na_copied = signal("na_copied", NA_PARTS)
        na_biased = signal("na_biased", 2 * H)
        na_max_made = signal("na_max_made", NA_PARTS)
        na_exp = signal("na_exp", 4 * H)
        na_recips = signal("na_recips", 2 * H)
        na_probs_made = signal("na_probs_made", 4 * H)
        na_keys_made = signal("na_keys_made", NA_PARTS)
        na_y_made = signal("na_y_made", 2 * H)
        mix_biased = signal("mix_biased", WT)
        mix_made = signal("mix_made", WT)
        rot_ctx = signal("rot_ctx", H)
        rot_mul = signal("rot_mul", 2 * H)
        rot_made = signal("rot_made", 2 * H)
        ret_v_made = signal("ret_v_made", 16)
        ret_g_made = signal("ret_g_made", RVT)
        ret_g_exp = signal("ret_g_exp", 4)
        ret_g_one = signal("ret_g_one", 4)
        ret_g_recip = signal("ret_g_recip", 4)
        ret_silu = signal("ret_silu", 4)
        decay_exp = signal("decay_exp", 2 * H)
        decay_masked = signal("decay_masked", 2 * H)
        decay_made = signal("decay_made", H)
        ret_decayed = signal("ret_decayed", 2 * H)
        ret_copied = signal("ret_copied", H)
        ret_centred = signal("ret_centred", H)
        ret_sq = signal("ret_sq", H)
        ret_log = signal("ret_log", H)
        ret_root = signal("ret_root", H)
        ret_normed = signal("ret_normed", H)
        ret_gated = signal("ret_gated", H)

        FREED2 = {name: (log_mean2, n) for name, n in ROOT.items()}
        for m in range(POSTS):
            for f in range(KD):
                FREED2[f"out{m}_{f}"] = (y2_squared, m * KD + f)
        for j in range(2):
            for f in range(FT):
                for n in range(2):
                    FREED2[f"conv{j}_{f}_{n}"] = (conv_made, (j * FT + f) * 2 + n)
        for f in range(2 * WT):
            FREED2[f"na_qk{f}"] = (na_qk_made, f)
        for f in range(4):
            FREED2[f"sgu_g{f}"], FREED2[f"sgu_u{f}"] = (sgu_copied, f), (sgu_copied, 4 + f)
            FREED2[f"na_v{f}"], FREED2[f"mix{f}"] = (na_v_made, f), (mix_biased, f)
        for n in range(NA_PARTS):
            FREED2[f"na_score{n}"], FREED2[f"na_keys{n}"] = (na_max_made, n), (na_keys_made, n)
        for n in range(2 * H):
            FREED2[f"na_pv{n}"] = (na_y_made, n)
        for f in range(2 * H):
            FREED2[f"ret_qk{f}"] = (rot_mul, f)
        for c in range(4):
            for b in range(4):
                FREED2[f"ret_v{c}_{b}"] = (ret_v_made, 4 * c + b)
        for f in range(RVT):
            FREED2[f"ret_g{f}"] = (ret_g_made, f)
        for h in range(H):
            FREED2[f"ret_score{h}_0"], FREED2[f"ret_score{h}_1"] = (ret_decayed, 2 * h), (ret_decayed, 2 * h + 1)
            FREED2[f"ret_o{h}"], FREED2[f"ret_mean{h}"] = (ret_copied, h), (ret_centred, h)
            FREED2[f"ret_var{h}"] = (ret_log, h)
        assert set(FREED2) == set(ORDER2)

        def bank2(name):
            return ps[:, GROUP2[name] % BANKS]

        def done2(name):
            return group2_done(GROUP2[name])

        def na_part(n, q):
            return 2 * n + q if n < H else H + n

        def halves_of(m):
            return ((slice(0, T), 1), (slice(T, T2), 2)) if m < 4 else ((slice(0, T), 1),)

        SQ_OF = [sq, wide_sq, wide_sq, ret_k, thin_sq]
        Y_OF = [wide_y, wide_y, thin_y, thin_y]
        YSQ_OF = [wide_sq, wide_sq, thin_sq, thin_sq]
        ret_squares = ret_e[:, 0:2, :]

        def gelu_part(c):
            b = (WT, WT + 2, 0, 2)[c]
            return sgu_in[:, b:b + 2, :].rearrange("p a b -> p (a b)")

        block = ctx.enter_context(nc.Block())

        @block.sync
        def _(sp):
            for s in range(RING):
                sp.dma_start(ring[:, s, :], tape[s]).then_inc(landed[s], 16)
            with sp.Fori(1, n_panels // RING) as turn:
                for s in range(RING):
                    sp.wait_ge(panel_used, turn * RING + (s - RING + 1))
                    sp.dma_start(ring[:, s, :], tape[bass.ds(turn * RING + s, 1), :, :].rearrange("a p n -> p (a n)"))\
                        .then_inc(landed[s], 16)
            sp.wait_ge(*x2_made(POSTS * KD - 1))
            sp.dma_start(out, xt).then_inc(stored, 16)
            sp.wait_ge(stored, 16)

        @block.tensor
        def _(pe):
            panel_at = [0, 0]
            entered = [False]
            layer = [0]

            def start_part(first_panel):
                panel_at[:] = [0, first_panel]

            def take(n):
                tile, first = panel_at
                col = tile % TILES_PER_PANEL
                slot = (first + tile // TILES_PER_PANEL) % RING
                if col == 0:
                    turn = (first + tile // TILES_PER_PANEL) // RING
                    pe.wait_ge(landed[slot], 16 * (turn + 1) + layer[0] * (16 * PANELS_1 // RING))
                    entered[0] = first + tile > 0
                assert col + n <= TILES_PER_PANEL
                panel_at[0] += n
                return ring[:, slot, col * TILE:(col + n) * TILE]

            def report(mm):
                if entered[0]:
                    mm.then_inc(panel_used, 1)
                    entered[0] = False

            def open_bank(name, l):
                g = GROUP[name]
                if g >= BANKS:
                    freed, n = FREED[ORDER[g - BANKS]]
                    pe.wait_ge(*freed(n, l))
                return bank(name)

            def linear(dst, moving):
                for k, m in enumerate(moving):
                    w = take(1)
                    mm = pe.matmul(dst, lhsT=w[:, 0:dst.shape[0]], rhs=m, start=(k == 0), stop=(k == len(moving) - 1))
                    if k < len(moving) - 1:
                        report(mm)
                return mm

            def stream(dsts, blocks):
                n = len(blocks[0])
                last = []
                for k in range(n):
                    w = take(4)
                    for b, dst in enumerate(dsts):
                        mm = pe.matmul(dst, lhsT=blocks[b][k], rhs=w, start=(k == 0), stop=(k == n - 1))
                        if k < n - 1:
                            report(mm)
                        else:
                            last.append(mm)
                return last

            def ada(n):
                for f in range(n):
                    j = ada_at[0]
                    ada_at[0] += 1
                    for k in range(KD):
                        mm = pe.matmul(ps[:, ADA_BANK, j * N_COND:(j + 1) * N_COND], lhsT=take(1), rhs=cond[:, k, :],
                                       start=(k == 0), stop=(k == KD - 1))
                        if j < N_ADA - 1 or k < KD - 1:
                            report(mm)
                return mm

            def stat(name, weight, parts, l):
                dst = open_bank(name, l)[:, 0:T]
                for k, (sig, n, part) in enumerate(parts):
                    pe.wait_ge(*sig(n, l))
                    mm = pe.matmul(dst, lhsT=const(weight), rhs=part, start=(k == 0), stop=(k == len(parts) - 1))
                mm.then_inc(group_done.sem, 1)

            ada_at = [0]
            pe.wait_ge(*prep(2))
            ada(N_ADA).then_inc(ada_done.sem, 1)

            with pe.Fori(0, DEPTH) as l:
                layer[0] = l
                start_part(ADA_PANELS)
                ada_at[0] = 0
                uk = [u1[:, k, :] for k in range(KD)]

                def rows(h):
                    return slice(64 * (h % 2), 64 * (h % 2) + 64)

                def project(name, moving, n_rows=P):
                    linear(open_bank(name, l)[0:n_rows, 0:T], moving).then_inc(group_done.sem, 1)

                def values(branch, src, n_k):
                    banks = [open_bank(f"{branch}_v{b}", l) for b in range(2)]
                    for mm in stream(banks, [[src[:, k, b * P:(b + 1) * P] for k in range(n_k)] for b in range(2)]):
                        mm.then_inc(group_done.sem, 1)

                pe.wait_ge(loaded["cst"], 16)
                stat("stat_mix", "mean_d", [(squared, k, sq[:, k, :]) for k in range(KD)], l)
                pe.wait_ge(*u_made(KD - 1, l))
                project("fox_f", uk, H)
                for f in range(2 * WT):
                    project(f"fox_qk{f}", uk)
                values("fox", u1, KD)
                for f in range(KQ + KKV):
                    project(f"lat{f}", uk)
                project("k_rope", uk)
                project("k_swap", uk)
                for f in range(2 * WT):
                    project(f"sb_qk{f}", uk)
                values("sb", u1, KD)

                stat("stat_q", "mean_q", [(lat_sq, k, sq[:, k, :]) for k in range(KQ)], l)
                stat("stat_kv", "mean_kv", [(lat_sq, KQ + k, sq[:, KQ + k, :]) for k in range(KKV)], l)
                cq = [latent[:, k, :] for k in range(KQ)]
                ckv = [latent[:, KQ + k, :] for k in range(KKV)]
                pe.wait_ge(*lat_norm(KQ - 1, l))
                for f in range(WT):
                    project(f"mla_q{f}", cq)
                for n in ("rope", "swap"):
                    for f in range(2):
                        project(f"q_{n}{f}", cq)
                pe.wait_ge(*lat_norm(KQ + KKV - 1, l))
                for f in range(WT):
                    project(f"mla_k{f}", ckv)
                values("mla", latent[:, KQ:KQ + KKV, :], KKV)

                def score(s):
                    b, h = divmod(s, H)
                    r, t = rows(h), h // 2
                    dst = open_bank(f"score{s}", l)
                    if b == 0:
                        pe.wait_ge(*qk_made(WT + t, l))
                        pe.wait_ge(*cum_made(0, l))
                        for q0, c0, n in ((0, 0, P), (P, P, T)):
                            pe.matmul(dst[:, c0:c0 + n], lhsT=fox_qk[r, t, q0:q0 + P], rhs=fox_qk[r, WT + t, 0:n],
                                      start=True, stop=False)
                            mm = pe.matmul(dst[:, c0:c0 + n], lhsT=const("ident")[0:H, h:h + 1].to_broadcast([H, P]),
                                           rhs=neg_cum[0:H, 0:n], start=False, stop=True)
                    elif b == 1:
                        rr, rt = slice(ROPE * (h % 4), ROPE * (h % 4) + ROPE), h // 4
                        pe.wait_ge(*nope_made(WT + t, l))
                        pe.wait_ge(*rope_made(2, l))
                        for q0, c0, n in ((0, 0, P), (P, P, T)):
                            pe.matmul(dst[:, c0:c0 + n], lhsT=mla_q[r, t, q0:q0 + P], rhs=mla_k[r, t, 0:n],
                                      start=True, stop=False)
                            mm = pe.matmul(dst[:, c0:c0 + n], lhsT=q_rope[rr, rt, q0:q0 + P], rhs=k_rope[rr, 0:n],
                                           start=False, stop=True)
                    else:
                        pe.wait_ge(*qk_made(3 * WT + t, l))
                        pe.matmul(dst[:, 0:T], lhsT=sb_qk[r, WT + t, 0:P], rhs=sb_qk[r, t, 0:T], start=True, stop=True)
                        mm = pe.matmul(dst[:, T:3 * P], lhsT=sb_qk[r, WT + t, P:T], rhs=sb_qk[r, t, P:T],
                                       start=True, stop=True)
                    mm.then_inc(group_done.sem, 1)

                def by_keys(s):
                    b, h = divmod(s, H)
                    dst = open_bank(f"keys{s}", l)
                    if b < 2:
                        pe.wait_ge(*probs_made(2 * s + 1, l))
                        for c in range(3):
                            mm = pe.transpose(dst[:, c * P:(c + 1) * P], probs[:, s % 3, c * P:(c + 1) * P],
                                              const("ident"))
                    else:
                        pe.wait_ge(*keep_masked(h, l))
                        keep = log_keep[:, s % 3, :]
                        pe.matmul(dst[:, 0:T], lhsT=const("after"), rhs=keep[:, 0:T], start=True, stop=False)
                        pe.matmul(dst[:, P:T], lhsT=const("ones"), rhs=keep[:, T:3 * P], start=False, stop=True)
                        mm = pe.matmul(dst[:, T:3 * P], lhsT=const("after"), rhs=keep[:, T:3 * P],
                                       start=True, stop=True)
                    mm.then_inc(group_done.sem, 1)

                def weighted_values(s):
                    b, h = divmod(s, H)
                    v = (fox_v, mla_v, sb_v)[b]
                    dst = open_bank(f"pv{s}", l)[rows(h), 0:T]
                    if s == 0:
                        pe.wait_ge(*v_made(5, l))
                    if b < 2:
                        pe.wait_ge(*keys_made(s, l))
                    else:
                        pe.wait_ge(*stick_made(h, l))
                    cols = slice(h * DH, (h + 1) * DH)
                    pe.matmul(dst, lhsT=v[:, 0, cols], rhs=keys[:, s % 2, 0:T], start=True, stop=False)
                    pe.matmul(dst[:, P:T], lhsT=v[:, 1, cols], rhs=keys[:, s % 2, T:3 * P], start=False, stop=True)\
                        .then_inc(group_done.sem, 1)

                def branch_out(b):
                    pe.wait_ge(*y_made((b + 1) * H - 1, l))
                    for f in range(KD):
                        project(f"branch{b}_{f}", [y[:, b * WT + k, :] for k in range(WT)])

                for i in range(STEPS + 2):
                    if i < STEPS:
                        score(i)
                        project(f"gate{i}", uk)
                    else:
                        branch_out(i - STEPS)
                    if 1 <= i <= STEPS:
                        by_keys(i - 1)
                    if i >= 2:
                        weighted_values(i - 2)
                branch_out(2)
                pe.wait_ge(*merged_made(2 * KD - 1, l))
                for f in range(KD):
                    project(f"w_out{f}", [merged[:, k, :] for k in range(KD)])

                ada(4)
                stat("stat_ffn", "mean_d", [(squared, KD + k, sq[:, k, :]) for k in range(KD)], l)
                pe.wait_ge(*u_made(2 * KD - 1, l))
                for f in range(FT):
                    project(f"ffn_gate{f}", uk)
                    project(f"ffn_up{f}", uk)
                    mm = ada(2)
                mm.then_inc(ada_done.sem, 1)
                for f in range(KD):
                    dst = open_bank(f"down{f}", l)[:, 0:T]
                    if f == 0:
                        pe.wait_ge(*hidden_made(FT - 1, l))
                    linear(dst, [hidden[:, k, :] for k in range(FT)]).then_inc(group_done.sem, 1)
                assert panel_at[0] == TILES_1

            layer[0] = 0

            def open2(name):
                g = GROUP2[name]
                if g >= BANKS:
                    freed, n = FREED2[ORDER2[g - BANKS]]
                    pe.wait_ge(*freed(n))
                return bank2(name)

            def project2(name, moving):
                n = moving[0].shape[-1]
                linear(open2(name)[:, 0:n], moving).then_inc(group2_done.sem, 1)

            def stat2(name, sig, m, src, n):
                dst = open2(name)[:, 0:n]
                for k in range(KD):
                    pe.wait_ge(*sig(m * KD + k))
                    mm = pe.matmul(dst, lhsT=const("mean_d"), rhs=src[:, k, 0:n], start=(k == 0), stop=(k == KD - 1))
                mm.then_inc(group2_done.sem, 1)

            def values2(names, c0=0):
                blocks = [[u[:, k, b * P:(b + 1) * P] for k in range(KD)] for b in range(4)]
                for mm in stream([open2(n) for n in names], blocks):
                    mm.then_inc(group2_done.sem, 1)

            def feed_forward2(j):
                m = 2 + 2 * j
                n = T2 if j == 0 else T
                stat2(f"norm{m}", squared2, m, SQ_OF[m], n)
                uk = [u[:, k, 0:n] for k in range(KD)]
                for f in range(FT):
                    for half in range(2):
                        if f == half == 0:
                            pe.wait_ge(*u2_made((m - 1) * KD + KD - 1))
                        project2(f"conv{j}_{f}_{half}", uk)
                    if j == 0:
                        mm = ada(2 if f < FT - 2 else 4)
                if j == 0:
                    mm.then_inc(ada_done.sem, 1)
                h = wide_hidden if j == 0 else thin_hidden
                pe.wait_ge(*hidden2_made(j * FT + FT - 1))
                for f in range(KD):
                    project2(f"out{1 + 2 * j}_{f}", [h[:, k, :] for k in range(FT)])
                stat2(f"post{1 + 2 * j}", y2_squared, 1 + 2 * j, YSQ_OF[1 + 2 * j], n)

            start_part(ADA_PANELS + DEPTH * PANELS_1)
            ada_at[0] = 0
            stat2("norm0", squared2, 0, SQ_OF[0], T)
            stat2("norm1", squared2, 1, SQ_OF[1], T2)
            pe.wait_ge(*u2_made(KD - 1))
            uk = [u[:, k, :] for k in range(KD)]
            for f in range(2 * WT):
                project2(f"na_qk{f}", uk)
            values2([f"sgu_g{b}" for b in range(4)])
            for f in range(WT):
                project2(f"sgu_u{f}", uk)
            values2([f"na_v{b}" for b in range(4)])

            def na_scores(n):
                h, r = n % H, slice(64 * (n % 2), 64 * (n % 2) + 64)
                q_t, k_t = na_qk[r, h // 2, :], na_qk[r, WT + h // 2, :]
                if n == 0:
                    pe.wait_ge(*na_qk_made(2 * WT - 1))
                if n < H:
                    for q in range(2):
                        dst = open2(f"na_score{na_part(n, q)}")
                        pe.matmul(dst, lhsT=q_t[:, q * P:(q + 1) * P], rhs=k_t, start=True, stop=True)\
                            .then_inc(group2_done.sem, 1)
                    return
                dst = open2(f"na_score{na_part(n, 0)}")
                for q in range(2):
                    mm = pe.matmul(dst[:, q * T:(q + 1) * T], lhsT=q_t[:, T + q * P:T + (q + 1) * P], rhs=k_t[:, T:T2],
                                   start=True, stop=True)
                mm.then_inc(group2_done.sem, 1)

            def na_by_keys(n):
                for q in range(2):
                    pe.wait_ge(*na_probs_made(2 * n + q))
                    if q == 0 or n < H:
                        dst = open2(f"na_keys{na_part(n, q)}")
                    for k in range(4 if n < H else 2):
                        c = k * P if n < H else k * T + q * P
                        mm = pe.transpose(dst[:, c:c + P], na_probs[:, n % 3, q, k * P:(k + 1) * P], const("ident"))
                    if q == 1 or n < H:
                        mm.then_inc(group2_done.sem, 1)

            def na_values(n):
                h, r = n % H, slice(64 * (n % 2), 64 * (n % 2) + 64)
                dst = open2(f"na_pv{n}")[r, 0:T]
                pe.wait_ge(*na_keys_made(na_part(n, 1 if n < H else 0)))
                if n == 0:
                    pe.wait_ge(*na_v_made(3))
                ks = range(4) if n < H else range(2)
                for k in ks:
                    mm = pe.matmul(dst, lhsT=na_v[:, k if n < H else 2 + k, h * DH:(h + 1) * DH], rhs=na_keys[:, n % 2, k, :],
                                   start=(k == 0), stop=(k == ks[-1]))
                mm.then_inc(group2_done.sem, 1)

            for i in range(2 * H + 2):
                if i < 2 * H:
                    na_scores(i)
                if 0 <= i - 1 < 2 * H:
                    na_by_keys(i - 1)
                if i >= 2:
                    na_values(i - 2)

            pe.wait_ge(*ln_made(3))
            pe.wait_ge(loaded["na"], 16 * 3)
            for t in range(WT):
                dst = open2(f"mix{t}")
                for b in range(4):
                    for g in range(2):
                        at = (2 * t + g) * DH
                        mm = pe.matmul(dst[64 * g:64 * g + 64, b * P:(b + 1) * P], lhsT=sgu_in[:, WT + b, at:at + DH],
                                       rhs=sgu_w[:, 2 * t + g, :], start=True, stop=True)
                mm.then_inc(group2_done.sem, 1)
            pe.wait_ge(*na_y_made(2 * H - 1))
            pe.wait_ge(*mix_made(WT - 1))
            for f in range(KD):
                project2(f"out0_{f}", [branches[:, k, :] for k in range(KD)])
            stat2("post0", y2_squared, 0, wide_sq, T2)
            feed_forward2(0)

            start_part(ADA_PANELS + DEPTH * PANELS_1 + PANELS_2[0])
            stat2("norm3", squared2, 3, SQ_OF[3], T2)
            pe.wait_ge(*u2_made(2 * KD + KD - 1))
            for f in range(2 * H):
                project2(f"ret_qk{f}", [u[:, k, 0:T if f < H else T2] for k in range(KD)])
            for c in range(4):
                values2([f"ret_v{c}_{b}" for b in range(4)])
            for f in range(RVT):
                project2(f"ret_g{f}", [u[:, k, 0:T] for k in range(KD)])

            def ret_scores(h):
                for b in range(2):
                    dst = open2(f"ret_score{h}_{b}")
                    if h == b == 0:
                        pe.wait_ge(*rot_made(2 * H - 1))
                        pe.wait_ge(*rot_ctx(H - 1))
                    for k in range(2):
                        at = (2 * b + k) * P
                        mm = pe.matmul(dst[:, k * T:(k + 1) * T], lhsT=ret_k[:, h, at:at + P], rhs=ret_q[:, h, :],
                                       start=True, stop=True)
                    mm.then_inc(group2_done.sem, 1)

            def ret_values(h):
                dst = open2(f"ret_o{h}")
                pe.wait_ge(*ret_decayed(2 * h + 1))
                if h == 0:
                    pe.wait_ge(*ret_v_made(15))
                for half in range(2):
                    for k in range(4):
                        at = h * RV + half * P
                        mm = pe.matmul(dst[:, half * T:(half + 1) * T], lhsT=ret_v[:, k, at:at + P],
                                       rhs=decayed[:, h % 2, k, :], start=(k == 0), stop=(k == 3))
                mm.then_inc(group2_done.sem, 1)

            def ret_mean(name, sig, h, src):
                dst = open2(f"{name}{h}")[:, 0:T]
                pe.wait_ge(*sig(h))
                for half in range(2):
                    mm = pe.matmul(dst, lhsT=const("mean_kv"), rhs=src[:, half, :], start=(half == 0), stop=(half == 1))
                mm.then_inc(group2_done.sem, 1)

            for i in range(H + 3):
                if i < H:
                    ret_scores(i)
                if 0 <= i - 1 < H:
                    ret_values(i - 1)
                if 0 <= i - 2 < H:
                    ret_mean("ret_mean", ret_copied, i - 2, ret_o[:, (i - 2) % 3])
                if 0 <= i - 3 < H:
                    ret_mean("ret_var", ret_sq, i - 3, ret_squares)
            pe.wait_ge(*ret_gated(H - 1))
            for f in range(KD):
                project2(f"out2_{f}", [ret_g[:, k, :] for k in range(RVT)])
            stat2("post2", y2_squared, 2, thin_sq, T)
            feed_forward2(1)

        @block.scalar
        def _(act):
            act.dma_start(cond[:, :, :], cond_in).then_inc(loaded["cond"], 16)
            act.dma_start(cst[:, :], consts).then_inc(loaded["cst"], 16)
            act.dma_start(par1_all[:, :, :], par1).then_inc(loaded["par1"], 16)
            act.dma_start(rope_t[:, 0, :].bitcast(I32), pos_in.partition_broadcast(P)).then_inc(loaded["pos"], 16)
            act.dma_start(xt, x_in).then_inc(loaded["x"], 16)
            act.dma_start(par2[:, :, :], par2_in).then_inc(loaded["par2"], 16)
            act.dma_start(misc[:, :], misc_in).then_inc(loaded["misc"], 16)
            act.dma_start(x[:, :, T:T2], ctx_in).then_inc(loaded["ctx"], 16)
            act.wait_ge(loaded["cond"], 16)
            act.activation(cond_e[:, :, :], cond[:, :, :], ACT.Exp, scale=-1.0).then_inc(prep_act.sem, 1)
            act.wait_ge(*prep(12))
            act.activation(rope_s[:, :], rope_t[:, 0, :], ACT.Sin).then_inc(prep_act.sem, 1)
            act.activation(rope_c[:, :], rope_t[:, 1, :], ACT.Sin).then_inc(prep_act.sem, 1)

            with act.Fori(0, DEPTH) as l:
                def squares(src):
                    for k in range(KD):
                        act.activation(sq[:, k, :], src[:, k, :], ACT.Square).then_inc(squared.sem, 1)

                def shifted(n, shift):
                    for k in range(KD):
                        act.wait_ge(*scaled(n * KD + k, l))
                        act.activation(u1[:, k, :], sq[:, k, :], ACT.Identity, bias=mod[:, shift * KD + k, 0:1])\
                            .then_inc(u_made.sem, 1)

                def queries_keys(branch, dst):
                    for f in range(2 * WT):
                        act.wait_ge(*done(f"{branch}_qk{f}", l))
                        act.activation(dst[:, f, :], bank(f"{branch}_qk{f}")[:, 0:T], ACT.Copy,
                                       scale=DH ** -0.5 if f < WT else 1.0).then_inc(qk_made.sem, 1)

                def inverse_rms(which, name):
                    dst = rstds[which % 3]
                    act.wait_ge(*done(name, l))
                    act.activation(dst, bank(name)[:, 0:T], ACT.Ln, bias=const("eps")).then_inc(log_mean.sem, 1)
                    act.wait_ge(*log_mean(which, l))
                    act.activation(dst, dst, ACT.Exp, scale=-0.5).then_inc(rstd_made.sem, 1)

                act.wait_ge(*mod_made(3, l))
                squares(xt)
                inverse_rms(0, "stat_mix")
                shifted(0, 0)

                act.wait_ge(*done("fox_f", l))
                act.activation(fox_l[0:H, :], bank("fox_f")[0:H, 0:T], ACT.Abs, bias=par_of("b_fox")[0:H, :])\
                    .then_inc(fox_soft.sem, 1)
                act.wait_ge(*fox_soft(0, l))
                act.activation(fox_l[0:H, :], fox_l[0:H, :], ACT.Exp, scale=-1.0).then_inc(fox_soft.sem, 1)
                act.wait_ge(*fox_soft(1, l))
                act.activation(fox_l[0:H, :], fox_l[0:H, :], ACT.Ln, bias=1.0).then_inc(fox_soft.sem, 1)
                queries_keys("fox", fox_qk)
                for f in range(KQ + KKV):
                    act.wait_ge(*done(f"lat{f}", l))
                    act.activation(latent[:, f, :], bank(f"lat{f}")[:, 0:T], ACT.Copy).then_inc(lat_made.sem, 1)
                    act.activation(sq[:, f, :], bank(f"lat{f}")[:, 0:T], ACT.Square).then_inc(lat_sq.sem, 1)
                queries_keys("sb", sb_qk)
                inverse_rms(1, "stat_q")
                inverse_rms(2, "stat_kv")
                for n, dst in enumerate((mla_q, mla_k)):
                    for f in range(WT):
                        name = f"mla_{'qk'[n]}{f}"
                        act.wait_ge(*done(name, l))
                        act.activation(dst[:, f, :], bank(name)[:, 0:T], ACT.Copy).then_inc(nope_made.sem, 1)

                halves = (slice(0, P), slice(P, 3 * P))

                def first_half(s):
                    b, h = divmod(s, H)
                    if b < 2:
                        for q, cols in enumerate(halves):
                            act.wait_ge(*max_made(2 * s + q, l))
                            act.activation(probs[:, s % 3, cols], probs[:, s % 3, cols], ACT.Exp,
                                           bias=neg_max[:, s, q:q + 1], accum_out=sums[:, s, q:q + 1])\
                                .then_inc(exp_made.sem, 1)
                        return
                    if h >= 3:
                        act.wait_ge(*beta_made(h - 3, l))
                    act.wait_ge(*done(f"score{s}", l))
                    z = soft[:, s % 3, :]
                    act.activation(z, bank(f"score{s}")[:, 0:3 * P], ACT.Abs).then_inc(z_soft.sem, 1)
                    act.wait_ge(*z_soft(3 * h, l))
                    act.activation(z, z, ACT.Exp, scale=-1.0).then_inc(z_soft.sem, 1)
                    act.wait_ge(*z_soft(3 * h + 1, l))
                    act.activation(z, z, ACT.Ln, bias=1.0).then_inc(z_soft.sem, 1)

                def second_half(s):
                    b, h = divmod(s, H)
                    if b < 2:
                        act.wait_ge(*done(f"keys{s}", l))
                        act.activation(keys[:, s % 2, :], bank(f"keys{s}")[:, 0:3 * P], ACT.Copy)\
                            .then_inc(keys_made.sem, 1)
                    else:
                        act.wait_ge(*stick_log(h, l))
                        act.activation(keys[:, s % 2, :], log_beta[:, s % 3, :], ACT.Exp).then_inc(stick_exp.sem, 1)

                for i in range(STEPS + 2):
                    if i < STEPS:
                        first_half(i)
                        act.wait_ge(*done(f"gate{i}", l))
                        act.activation(sigma[:, i, :], bank(f"gate{i}")[:, 0:T], ACT.Exp, scale=-1.0)\
                            .then_inc(gate_exp.sem, 1)
                    if 1 <= i <= STEPS:
                        second_half(i - 1)
                    if i >= 2:
                        b, h = divmod(i - 2, H)
                        r = slice(64 * (h % 2), 64 * (h % 2) + 64)
                        act.wait_ge(*done(f"pv{i - 2}", l))
                        act.activation(y[r, b * WT + h // 2, :], bank(f"pv{i - 2}")[r, 0:T], ACT.Copy)\
                            .then_inc(y_made.sem, 1)

                for k in range(KD):
                    act.wait_ge(*x_mixed(k, l))
                    act.activation(sq[:, k, :], xt[:, k, :], ACT.Square).then_inc(squared.sem, 1)
                inverse_rms(3, "stat_ffn")
                shifted(1, 3)
                for f in range(FT):
                    act.wait_ge(*done(f"ffn_gate{f}", l))
                    if f >= 3:
                        act.wait_ge(*ffn_recip(f - 3, l))
                    act.activation(ffn_e[:, f % 3, :], bank(f"ffn_gate{f}")[:, 0:T], ACT.Exp, scale=-1.0)\
                        .then_inc(ffn_exp.sem, 1)

            def inverse_rms2(name, dst):
                act.wait_ge(*done2(name))
                act.activation(dst, bank2(name)[:, 0:dst.shape[-1]], ACT.Ln, bias=const("eps")).then_inc(log_mean2.sem, 1)
                act.wait_ge(*log_mean2(ROOT[name]))
                act.activation(dst, dst, ACT.Exp, scale=-0.5).then_inc(rstd2_made.sem, 1)

            def norm_in(m, ready, chunk):
                n = T if m in (0, 4) else T2
                for k in range(KD):
                    act.wait_ge(*ready(k))
                    act.activation(SQ_OF[m][:, k, 0:n], x[:, k, 0:n], ACT.Square).then_inc(squared2.sem, 1)
                inverse_rms2(f"norm{m}", rstd2[:, 0:n])
                if chunk is None:
                    return
                for k in range(KD):
                    act.wait_ge(*scaled2(m * KD + k))
                    for cols, c in halves_of(m):
                        a = act.activation(u[:, k, cols], SQ_OF[m][:, k, cols], ACT.Identity,
                                           bias=mod[:, chunk * KD + k, c:c + 1])
                    a.then_inc(u2_made.sem, 1)

            def norm_out(m):
                n = T2 if m < 2 else T
                for f in range(KD):
                    act.wait_ge(*done2(f"out{m}_{f}"))
                    src = bank2(f"out{m}_{f}")[:, 0:n]
                    act.activation(Y_OF[m][:, f, :], src, ACT.Copy).then_inc(y2_copied.sem, 1)
                    act.activation(YSQ_OF[m][:, f, :], src, ACT.Square).then_inc(y2_squared.sem, 1)
                inverse_rms2(f"post{m}", rstd2[:, 0:n])

            def feed_forward2(j):
                n, conv = (T2, wide_conv) if j == 0 else (T, thin_conv)

                def gate_exp2(f):
                    g = j * FT + f
                    act.wait_ge(*conv_made(2 * g))
                    if f >= 2:
                        act.wait_ge(*conv_silu(g - 2))
                    act.activation(conv[:, 2, f % 2, :], conv[:, 0, f % 2, :], ACT.Exp, scale=-1.0)\
                        .then_inc(conv_exp.sem, 1)

                for f in range(FT + 1):
                    if f < FT:
                        for half in range(2):
                            g = j * FT + f
                            if f >= 2 and half == 0:
                                act.wait_ge(*hidden2_made(g - 2))
                            act.wait_ge(*done2(f"conv{j}_{f}_{half}"))
                            at = half * FT + f
                            act.activation(conv[:, half, f % 2, :], bank2(f"conv{j}_{f}_{half}")[:, 0:n], ACT.Identity,
                                           scale=par2_of(j, "conv_w", 2 * FT + at, 1), bias=par2_of(j, "conv_b", at, 1))\
                                .then_inc(conv_mid.sem, 1)
                    if f >= 1:
                        gate_exp2(f - 1)

            act.wait_ge(*x_done(KD - 1, DEPTH - 1))
            act.dma_start(na_bias, bias_in).then_inc(loaded["na"], 16)
            act.dma_start(sgu_w, sgu_w_in).then_inc(loaded["na"], 16)
            act.dma_start(sgu_b, sgu_b_in).then_inc(loaded["na"], 16)
            act.dma_start(rope_c[:, :], axial[:, 0, :]).then_inc(loaded["axial"], 16)
            act.dma_start(rope_s[:, :], axial[:, 1, :]).then_inc(loaded["axial"], 16)

            norm_in(0, lambda k: x_done(k, DEPTH - 1), None)
            act.wait_ge(loaded["ctx"], 16)
            norm_in(1, lambda k: scaled2(k), 0)
            for f in range(2 * WT):
                act.wait_ge(*done2(f"na_qk{f}"))
                act.activation(na_qk[:, f, :], bank2(f"na_qk{f}"), ACT.Copy, scale=DH ** -0.5 if f < WT else 1.0)\
                    .then_inc(na_qk_made.sem, 1)

            def gelu(c):
                part, t = gelu_part(c), sgu_t[:, c % 2, :]
                if c >= 2:
                    act.wait_ge(*gelu_made(c - 2))
                act.activation(t, part, ACT.Square).then_inc(gelu_sq.sem, 1)
                act.wait_ge(*gelu_in(c))
                act.activation(t, t, ACT.Exp, scale=-2.0 * (2.0 / np.pi) ** 0.5).then_inc(gelu_exp.sem, 1)

            for half, name in enumerate(("sgu_g", "sgu_u")):
                for f in range(4):
                    act.wait_ge(*done2(f"{name}{f}"))
                    act.activation(sgu_in[:, WT + f if half == 0 else f, :], bank2(f"{name}{f}"), ACT.Copy)\
                        .then_inc(sgu_copied.sem, 1)
                    if f % 2 == 1:
                        act.wait_ge(*sgu_copied(4 * half + f))
                        gelu(2 * half + f // 2)
                if half == 0:
                    for b in range(4):
                        act.wait_ge(*ln_steps(2 + b))
                        act.activation(sgu_t[:, b // 2, (b % 2) * W:(b % 2 + 1) * W], sgu_in[:, WT + b, :], ACT.Square, accum_out=ln_var[:, b:b + 1])\
                            .then_inc(ln_sq.sem, 1)
                    act.wait_ge(*ln_sq(3))
                    act.activation(ln_rstd, ln_var, ACT.Ln, scale=1.0 / W, bias=const("eps")).then_inc(ln_root.sem, 1)
                    act.wait_ge(*ln_root(0))
                    act.activation(ln_rstd, ln_rstd, ACT.Exp, scale=-0.5).then_inc(ln_root.sem, 1)
            for b in range(4):
                act.wait_ge(*done2(f"na_v{b}"))
                act.activation(na_v[:, b, :], bank2(f"na_v{b}"), ACT.Copy).then_inc(na_v_made.sem, 1)

            def na_softmax(n):
                p = na_probs[:, n % 3]
                for q in range(2):
                    if q == 0 or n < H:
                        part = na_part(n, q)
                        if n >= 3:
                            act.wait_ge(*done2(f"na_keys{na_part(n - 3, 1 if n - 3 < H else 0)}"))
                        act.wait_ge(*done2(f"na_score{part}"))
                        src = bank2(f"na_score{part}")
                        if n < H:
                            act.activation(p[:, q, T:T2], src[:, T:T2], ACT.Copy).then_inc(na_copied.sem, 1)
                        else:
                            act.activation(p[:, :, 0:T], src.rearrange("p (q k) -> p q k", q=2), ACT.Copy)\
                                .then_inc(na_copied.sem, 1)
                for q in range(2):
                    act.wait_ge(*na_max_made(na_part(n, q if n < H else 0)))
                    cols = slice(0, T2 if n < H else T)
                    act.activation(p[:, q, cols], p[:, q, cols], ACT.Exp, bias=na_max[:, n, q:q + 1],
                                   accum_out=na_sum[:, n, q:q + 1]).then_inc(na_exp.sem, 1)

            for i in range(2 * H + 2):
                if i < 2 * H:
                    na_softmax(i)
                n = i - 1
                if 0 <= n < 2 * H:
                    for q in range(2 if n < H else 1):
                        name = f"na_keys{na_part(n, q)}"
                        act.wait_ge(*done2(name))
                        if n < H:
                            act.activation(na_keys[:, n % 2, :, q * P:(q + 1) * P],
                                           bank2(name).rearrange("p (k q) -> p k q", k=4), ACT.Copy).then_inc(na_keys_made.sem, 1)
                        else:
                            act.activation(na_keys[:, n % 2, 0:2, :], bank2(name).rearrange("p (k q) -> p k q", k=2), ACT.Copy)\
                                .then_inc(na_keys_made.sem, 1)
                if i >= 2:
                    n = i - 2
                    h, r = n % H, slice(64 * (n % 2), 64 * (n % 2) + 64)
                    act.wait_ge(*done2(f"na_pv{n}"))
                    act.activation(branches[r, h // 2, 0:T] if n < H else branches[r, h // 2, T:T2],
                                   bank2(f"na_pv{n}")[r, 0:T], ACT.Copy).then_inc(na_y_made.sem, 1)
            norm_out(0)
            norm_in(2, lambda k: x2_made(k), 3)
            feed_forward2(0)
            norm_out(1)

            act.wait_ge(*x2_made(2 * KD - 1))
            act.dma_start(ret_mask, mask_in).then_inc(loaded["mask"], 16)
            norm_in(3, lambda k: x2_made(KD + k), 0)
            act.wait_ge(*u2_made(3 * KD - 1))
            act.dma_start(ret_dist, dist_in).then_inc(loaded["dist"], 16)
            for h in range(H):
                act.wait_ge(*done2(f"ret_qk{H + h}"))
                act.activation(ret_k[:, h, T:T2], bank2(f"ret_qk{H + h}")[:, T:T2], ACT.Copy).then_inc(rot_ctx.sem, 1)
            for c in range(4):
                for b in range(4):
                    act.wait_ge(*done2(f"ret_v{c}_{b}"))
                    act.activation(ret_v[:, b, c * 512:(c + 1) * 512], bank2(f"ret_v{c}_{b}"), ACT.Copy)\
                        .then_inc(ret_v_made.sem, 1)

            def decay_powers(h):
                act.wait_ge(loaded["dist"], 16)
                for d, dst in enumerate((decay[:, h % 2], decay_b)):
                    if d == 0 and h >= 2:
                        act.wait_ge(*ret_decayed(2 * (h - 2) + 1))
                    if d == 1 and h >= 1:
                        act.wait_ge(*decay_made(h - 1))
                    act.activation(dst, ret_dist[:, 4 * d:4 * d + 4, :], ACT.Exp,
                                   scale=misc_of("log_decay")[:, d * H + h:d * H + h + 1]).then_inc(decay_exp.sem, 1)

            decay_powers(0)
            for f in range(RVT):
                act.wait_ge(*done2(f"ret_g{f}"))
                act.activation(ret_g[:, f, :], bank2(f"ret_g{f}")[:, 0:T], ACT.Copy).then_inc(ret_g_made.sem, 1)
            for c in range(4):
                act.wait_ge(*ret_g_made(RVT - 1))
                act.activation(ret_e[:, 4 * c:4 * c + 4, :], ret_g[:, 4 * c:4 * c + 4, :], ACT.Exp, scale=-1.0)\
                    .then_inc(ret_g_exp.sem, 1)
            for i in range(H + 3):
                if i + 1 < H:
                    decay_powers(i + 1)
                if 0 <= i - 1 < H:
                    h = i - 1
                    act.wait_ge(*done2(f"ret_o{h}"))
                    if h >= 3:
                        act.wait_ge(*ret_gated(h - 3))
                    act.activation(ret_o[:, h % 3], bank2(f"ret_o{h}").rearrange("p (a t) -> p a t", a=2), ACT.Copy)\
                        .then_inc(ret_copied.sem, 1)
                if 0 <= i - 2 < H:
                    h = i - 2
                    act.wait_ge(*ret_centred(h))
                    if h == 0:
                        act.wait_ge(*ret_silu(3))
                    if h >= 1:
                        act.wait_ge(*done2(f"ret_var{h - 1}"))
                    act.activation(ret_squares, ret_o[:, h % 3], ACT.Square).then_inc(ret_sq.sem, 1)
                if 0 <= i - 3 < H:
                    h = i - 3
                    act.wait_ge(*done2(f"ret_var{h}"))
                    if h >= 2:
                        act.wait_ge(*ret_normed(h - 2))
                    act.activation(ret_rstd[:, h % 2, :], bank2(f"ret_var{h}")[:, 0:T], ACT.Ln, bias=const("eps"))\
                        .then_inc(ret_log.sem, 1)
                    act.wait_ge(*ret_log(h))
                    act.activation(ret_rstd[:, h % 2, :], ret_rstd[:, h % 2, :], ACT.Exp, scale=-0.5).then_inc(ret_root.sem, 1)
            norm_out(2)
            norm_in(4, lambda k: x2_made(2 * KD + k), 3)
            feed_forward2(1)
            norm_out(3)

        @block.vector
        def _(dve):
            dve.wait_ge(*prep_act(0))
            dve.tensor_scalar(cond_e[:, :, :], cond_e[:, :, :], 1.0, None, ALU.add).then_inc(prep.sem, 1)
            dve.wait_ge(*prep(0))
            dve.reciprocal(cond_r[:, :, :], cond_e[:, :, :]).then_inc(prep.sem, 1)
            dve.wait_ge(*prep(1))
            dve.tensor_tensor(cond[:, :, :], cond[:, :, :], cond_r[:, :, :], ALU.mult).then_inc(prep.sem, 1)

            turn = 2 * np.pi
            part1 = 6.28125
            part2 = float(np.float32(np.round((turn - part1) * 2 ** 20) / 2 ** 20))
            part3 = float(turn - part1 - part2)
            whole = 1.5 * 2 ** 23
            pos, ang, kk = rope_t[:, 0, :], rope_t[:, 1, :], rope_c[:, :]
            dve.wait_ge(loaded["pos"], 16)
            dve.wait_ge(loaded["cst"], 16)
            dve.tensor_copy(rope_s[:, :], pos.bitcast(I32)).then_inc(prep.sem, 1)
            dve.wait_ge(*prep(3))
            dve.tensor_scalar(ang, rope_s[:, :], const("inv_freq"), None, ALU.mult).then_inc(prep.sem, 1)
            dve.wait_ge(*prep(4))
            dve.tensor_scalar(kk, ang, 1.0 / turn, whole, ALU.mult, ALU.add).then_inc(prep.sem, 1)
            dve.wait_ge(*prep(5))
            dve.tensor_scalar(kk, kk, whole, None, ALU.subtract).then_inc(prep.sem, 1)
            for n, part in enumerate((part1, part2, part3)):
                dve.wait_ge(*prep(6 + n))
                dve.scalar_tensor_tensor(ang, kk, -part, ang, ALU.mult, ALU.add).then_inc(prep.sem, 1)
            dve.wait_ge(*prep(9))
            dve.tensor_scalar(pos, ang, 3.1415925, -3.1415925, ALU.min, ALU.max).then_inc(prep.sem, 1)
            dve.wait_ge(*prep(10))
            dve.tensor_scalar(ang, pos, 0.5, None, ALU.mult).then_inc(prep.sem, 1)
            dve.memset(recips[:, :, :], 0.0).then_inc(prep.sem, 1)
            dve.wait_ge(*prep_act(2))
            dve.tensor_tensor(rope_c[:, :], rope_c[:, :], rope_c[:, :], ALU.mult).then_inc(prep.sem, 1)
            dve.wait_ge(*prep(13))
            dve.tensor_scalar(rope_c[:, :], rope_c[:, :], -2.0, 1.0, ALU.mult, ALU.add).then_inc(prep.sem, 1)
            dve.tensor_scalar(rope_s[:, :], rope_s[:, :], const("rope_sign"), None, ALU.mult).then_inc(prep.sem, 1)
            dve.wait_ge(loaded["par1"], 16)
            dve.wait_ge(loaded["x"], 16)
            dve.wait_ge(*prep(15))

            with dve.Fori(0, DEPTH) as l:
                def scale_x(n, gain):
                    for k in range(KD):
                        dve.scalar_tensor_tensor(sq[:, k, :], xt[:, k, :], gain[:, k:k + 1], rstds[0],
                                                 ALU.mult, ALU.mult)\
                            .then_inc(scaled.sem, 1)

                def values(n, branch, dst):
                    for b in range(2):
                        dve.wait_ge(*done(f"{branch}_v{b}", l))
                        dve.tensor_copy(dst[:, b, :], bank(f"{branch}_v{b}")).then_inc(v_made.sem, 1)

                def rotate(n, straight, swapped, dst):
                    for j, (name, table) in enumerate(((straight, rope_c), (swapped, rope_s))):
                        dve.wait_ge(*done(name, l))
                        if n:
                            dve.wait_ge(*rope_made(n - 1, l))
                        dve.tensor_tensor(rope_t[:, j, :], bank(name)[:, 0:T], table[:, :], ALU.mult)\
                            .then_inc(rope_mul.sem, 1)
                    dve.wait_ge(*rope_mul(2 * n + 1, l))
                    dve.tensor_tensor(dst, rope_t[:, 0, :], rope_t[:, 1, :], ALU.add).then_inc(rope_made.sem, 1)

                dve.tensor_copy(par[:, :], par1_all[:, bass.ds(l, 1), :].rearrange("p a n -> p (a n)"))\
                    .then_inc(mod_made.sem, 1)
                dve.wait_ge(*mod_made(0, l))
                dve.wait_ge(*ada_done(0, l))
                dve.tensor_tensor(mod[:, :, :],
                                  ps[:, ADA_BANK, 0:N_ADA * N_COND].rearrange("p (j c) -> p j c", c=N_COND),
                                  par_of("b_ada").unsqueeze(2).to_broadcast([P, N_ADA, N_COND]), ALU.add)\
                    .then_inc(mod_made.sem, 1)
                dve.wait_ge(*mod_made(1, l))
                for gain, g, chunk in ((gs_mix, "g_mix", 1), (gs_ffn, "g_ffn", 4)):
                    dve.scalar_tensor_tensor(gain[:, :], mod[:, chunk * KD:(chunk + 1) * KD, 0], 1.0, par_of(g),
                                             ALU.add, ALU.mult).then_inc(mod_made.sem, 1)
                dve.wait_ge(*mod_made(3, l))

                dve.wait_ge(*rstd_made(0, l))
                scale_x(0, gs_mix)

                dve.wait_ge(*done("fox_f", l))
                dve.wait_ge(*fox_soft(0, l))
                dve.tensor_scalar(fox_t[0:H, :], bank("fox_f")[0:H, 0:T], par_of("b_fox")[0:H, :], 0.0, ALU.add, ALU.min)\
                    .then_inc(fox_low.sem, 1)
                dve.wait_ge(*fox_low(0, l))
                dve.wait_ge(*fox_soft(2, l))
                dve.tensor_tensor_scan(neg_cum[0:H, :], fox_l[0:H, :], fox_t[0:H, :], 0.0, ALU.add, ALU.subtract)\
                    .then_inc(cum_made.sem, 1)
                values(0, "fox", fox_v)
                rotate(0, "k_rope", "k_swap", k_rope)
                values(1, "sb", sb_v)
                for which, g, k0, n in ((1, "g_q", 0, KQ), (2, "g_kv", KQ, KKV)):
                    dve.wait_ge(*rstd_made(which, l))
                    for k in range(n):
                        dve.wait_ge(*lat_made(k0 + k, l))
                        dve.scalar_tensor_tensor(latent[:, k0 + k, :], latent[:, k0 + k, :], par_of(g)[:, k:k + 1],
                                                 rstds[which % 3],
                                                 ALU.mult, ALU.mult).then_inc(lat_norm.sem, 1)
                for f in range(2):
                    rotate(1 + f, f"q_rope{f}", f"q_swap{f}", q_rope[:, f, :])
                values(2, "mla", mla_v)

                halves = (slice(0, P), slice(P, 3 * P))

                def logits(s):
                    b, h = divmod(s, H)
                    src = bank(f"score{s}")[:, 0:3 * P]
                    if b < 2:
                        if s >= 3:
                            dve.wait_ge(*done(f"keys{s - 3}", l))
                        dve.wait_ge(*done(f"score{s}", l))
                        dve.scalar_tensor_tensor(probs[:, s % 3, :], src, 1.0 if b == 0 else (DH + ROPE) ** -0.5,
                                                 const("mask_fox" if b == 0 else "mask_mla"), ALU.mult, ALU.add)\
                            .then_inc(masked.sem, 1)
                        dve.wait_ge(*masked(s, l))
                        for q, cols in enumerate(halves):
                            dve.tensor_reduce(neg_max[:, s, q:q + 1], probs[:, s % 3, cols], AX.X, ALU.max, negate=True)\
                                .then_inc(max_made.sem, 1)
                        return
                    dve.wait_ge(*z_soft(3 * h + 2, l))
                    if h >= 3:
                        dve.wait_ge(*stick_exp(h - 3, l))
                        dve.wait_ge(*done(f"keys{s - 3}", l))
                    dve.scalar_tensor_tensor(log_beta[:, s % 3, :], src, 0.0, soft[:, s % 3, :], ALU.min, ALU.subtract)\
                        .then_inc(beta_made.sem, 1)
                    dve.wait_ge(*beta_made(h, l))
                    dve.tensor_tensor(log_keep[:, s % 3, :], log_beta[:, s % 3, :], src, ALU.subtract)\
                        .then_inc(keep_made.sem, 1)

                def normalise(s):
                    dve.wait_ge(*exp_made(2 * s + 1, l))
                    dve.reciprocal(recips[:, s, :], sums[:, s, :]).then_inc(recip_made.sem, 1)
                    dve.wait_ge(*recip_made(s, l))
                    for q, cols in enumerate(halves):
                        dve.tensor_scalar(probs[:, s % 3, cols], probs[:, s % 3, cols], recips[:, s, q:q + 1], None,
                                          ALU.mult).then_inc(probs_made.sem, 1)

                def gate_sigma(s):
                    dve.wait_ge(*gate_one(s, l))
                    dve.reciprocal(sigma[:, s, :], sigma[:, s, :]).then_inc(sigma_made.sem, 1)

                def branch_gate(b):
                    for f in range(KD):
                        dve.wait_ge(*done(f"branch{b}_{f}", l))
                        if b == 0:
                            if f == 0:
                                dve.wait_ge(*sigma_made(STEPS - 1, l))
                            dve.tensor_tensor(merged[:, f, :], bank(f"branch0_{f}")[:, 0:T], sigma[:, f, :], ALU.mult)\
                                .then_inc(gated_made.sem, 1)
                            continue
                        n = (b - 1) * KD + f
                        if n >= 2:
                            dve.wait_ge(*merged_made(n - 2, l))
                        dve.tensor_tensor(gated[:, n % 2, :], bank(f"branch{b}_{f}")[:, 0:T], sigma[:, b * KD + f, :],
                                          ALU.mult).then_inc(gated_made.sem, 1)

                for i in range(STEPS + 2):
                    if i < STEPS:
                        logits(i)
                    if 1 <= i <= STEPS:
                        gate_sigma(i - 1)
                    if i < 2 * H:
                        normalise(i)
                    if i >= STEPS:
                        branch_gate(i - STEPS)
                    if 2 * H < i <= STEPS:
                        s = i - 1
                        dve.wait_ge(*done(f"keys{s}", l))
                        dve.tensor_tensor(log_beta[:, s % 3, :], log_beta[:, s % 3, :], bank(f"keys{s}")[:, 0:3 * P],
                                          ALU.add).then_inc(stick_log.sem, 1)
                branch_gate(2)

                for f in range(KD):
                    dve.wait_ge(*done(f"w_out{f}", l))
                    dve.scalar_tensor_tensor(xt[:, f, :], bank(f"w_out{f}")[:, 0:T], mod[:, 2 * KD + f, 0:1], xt[:, f, :],
                                             ALU.mult, ALU.add).then_inc(x_mixed.sem, 1)
                dve.wait_ge(*rstd_made(3, l))
                dve.wait_ge(*x_mixed(KD - 1, l))
                scale_x(1, gs_ffn)
                for f in range(FT):
                    slot = f % 3
                    dve.wait_ge(*ffn_one(f, l))
                    dve.reciprocal(ffn_r[:, slot, :], ffn_e[:, slot, :]).then_inc(ffn_recip.sem, 1)
                    dve.wait_ge(*ffn_recip(f, l))
                    dve.tensor_tensor(ffn_gu[:, slot, :], ffn_r[:, slot, :], bank(f"ffn_gate{f}")[:, 0:T], ALU.mult)\
                        .then_inc(ffn_prod.sem, 1)
                    dve.wait_ge(*ffn_prod(f, l))
                    dve.wait_ge(*done(f"ffn_up{f}", l))
                    dve.tensor_tensor(hidden[:, f, :], ffn_gu[:, slot, :], bank(f"ffn_up{f}")[:, 0:T], ALU.mult)\
                        .then_inc(hidden_made.sem, 1)
                for f in range(KD):
                    dve.wait_ge(*done(f"down{f}", l))
                    dve.scalar_tensor_tensor(xt[:, f, :], bank(f"down{f}")[:, 0:T], mod[:, 5 * KD + f, 0:1], xt[:, f, :],
                                             ALU.mult, ALU.add).then_inc(x_done.sem, 1)

            def layer_gains(j):
                dve.wait_ge(*ada_done(0, DEPTH + j))
                dve.tensor_tensor(mod[:, :, :],
                                  ps[:, ADA_BANK, 0:N_ADA * N_COND].rearrange("p (j c) -> p j c", c=N_COND),
                                  par2_of(j, "b_ada").unsqueeze(2).to_broadcast([P, N_ADA, N_COND]), ALU.add)\
                    .then_inc(mod2_made.sem, 1)
                dve.wait_ge(*mod2_made(9 * j))
                for n, chunk in enumerate((1, 2, 4, 5)):
                    for c in range(2):
                        m, g = mod[:, chunk * KD:(chunk + 1) * KD, 1 + c], par2_of(j, "norm_g", n * KD, KD)
                        if n % 2 == 0:
                            a = dve.scalar_tensor_tensor(gains[:, n, c, :], m, 1.0, g, ALU.add, ALU.mult)
                        else:
                            a = dve.tensor_tensor(gains[:, n, c, :], m, g, ALU.mult)
                        a.then_inc(mod2_made.sem, 1)
                dve.wait_ge(*mod2_made(9 * j + 8))

            def norm_in(m, kind):
                dve.wait_ge(*rstd2_made(ROOT[f"norm{m}"]))
                for k in range(KD):
                    if m == 0:
                        dve.scalar_tensor_tensor(xt[:, k, :], xt[:, k, :], misc_of("g_final")[:, k:k + 1], rstd2[:, 0:T],
                                                 ALU.mult, ALU.mult).then_inc(scaled2.sem, 1)
                        continue
                    for cols, c in halves_of(m):
                        a = dve.scalar_tensor_tensor(SQ_OF[m][:, k, cols], x[:, k, cols], gains[:, kind, c - 1, k:k + 1],
                                                     rstd2[:, cols], ALU.mult, ALU.mult)
                    a.then_inc(scaled2.sem, 1)

            def norm_out(m, kind):
                dve.wait_ge(*rstd2_made(ROOT[f"post{m}"]))
                for k in range(KD):
                    for cols, c in halves_of(1 if m < 2 else 4):
                        a = dve.scalar_tensor_tensor(Y_OF[m][:, k, cols], Y_OF[m][:, k, cols], gains[:, kind, c - 1, k:k + 1],
                                                     rstd2[:, cols], ALU.mult, ALU.mult)
                    a.then_inc(y2_scaled.sem, 1)

            def feed_forward2(j):
                n, conv, h = (T2, wide_conv, wide_hidden) if j == 0 else (T, thin_conv, thin_hidden)
                spans = n // T

                def taps(f):
                    for half in range(2):
                        g = 2 * (j * FT + f) + half
                        at = half * FT + f
                        src = bank2(f"conv{j}_{f}_{half}")[:, 0:n].rearrange("p (s t) -> p s t", s=spans)
                        dst = conv[:, half, f % 2, :].rearrange("p (s t) -> p s t", s=spans)
                        dve.wait_ge(*conv_mid(g))
                        dve.scalar_tensor_tensor(dst[:, :, 1:T], src[:, :, 0:T - 1], par2_of(j, "conv_w", at, 1),
                                                 dst[:, :, 1:T], ALU.mult, ALU.add).then_inc(conv_left.sem, 1)
                        dve.wait_ge(*conv_left(g))
                        dve.scalar_tensor_tensor(dst[:, :, 0:T - 1], src[:, :, 1:T], par2_of(j, "conv_w", 4 * FT + at, 1),
                                                 dst[:, :, 0:T - 1], ALU.mult, ALU.add).then_inc(conv_made.sem, 1)

                def glu(f):
                    g = j * FT + f
                    e, gate, up = conv[:, 2, f % 2, :], conv[:, 0, f % 2, :], conv[:, 1, f % 2, :]
                    dve.wait_ge(*conv_one(g))
                    dve.reciprocal(e, e).then_inc(conv_recip.sem, 1)
                    dve.wait_ge(*conv_recip(g))
                    dve.tensor_tensor(gate, gate, e, ALU.mult).then_inc(conv_silu.sem, 1)
                    dve.wait_ge(*conv_silu(g))
                    dve.tensor_tensor(h[:, f, :], gate, up, ALU.mult).then_inc(hidden2_made.sem, 1)

                for f in range(FT + 1):
                    if f < FT:
                        taps(f)
                    if f >= 1:
                        glu(f - 1)

            dve.wait_ge(loaded["misc"], 16)
            dve.wait_ge(loaded["par2"], 16)
            dve.wait_ge(*x_done(KD - 1, DEPTH - 1))
            layer_gains(0)
            norm_in(0, None)
            norm_in(1, 0)

            def gelu(c):
                part, t = gelu_part(c), sgu_t[:, c % 2, :]
                dve.wait_ge(*gelu_poly(2 * c + 1))
                dve.tensor_tensor(t, t, part, ALU.mult).then_inc(gelu_in.sem, 1)
                dve.wait_ge(*gelu_one(c))
                dve.reciprocal(t, t).then_inc(gelu_recip.sem, 1)
                dve.wait_ge(*gelu_recip(c))
                dve.tensor_tensor(part, part, t, ALU.mult).then_inc(gelu_made.sem, 1)

            gelu(0)
            gelu(1)
            dve.wait_ge(*gelu_made(1))
            gating = sgu_in[:, WT:2 * WT, :]
            dve.tensor_reduce(ln_sum, gating, AX.X, ALU.add).then_inc(ln_steps.sem, 1)
            dve.wait_ge(*ln_steps(0))
            dve.tensor_scalar(ln_sum, ln_sum, 1.0 / W, None, ALU.mult).then_inc(ln_steps.sem, 1)
            dve.wait_ge(*ln_steps(1))
            for b in range(4):
                dve.tensor_scalar(gating[:, b, :], gating[:, b, :], ln_sum[:, b:b + 1], None, ALU.subtract)\
                    .then_inc(ln_steps.sem, 1)
            dve.wait_ge(*ln_root(1))
            for b in range(4):
                dve.tensor_scalar(gating[:, b, :], gating[:, b, :], ln_rstd[:, b:b + 1], None, ALU.mult)\
                    .then_inc(ln_made.sem, 1)
            gelu(2)
            gelu(3)

            def na_softmax(n):
                p = na_probs[:, n % 3]
                if n >= 3:
                    dve.wait_ge(*done2(f"na_keys{na_part(n - 3, 1 if n - 3 < H else 0)}"))
                if n == 0:
                    dve.wait_ge(*bias_masked(1))
                for q in range(2 if n < H else 1):
                    part = na_part(n, q)
                    if n < H:
                        dve.wait_ge(*done2(f"na_score{part}"))
                        dve.wait_ge(*na_copied(part))
                        dve.tensor_tensor(p[:, q, 0:T], bank2(f"na_score{part}")[:, 0:T], na_bias[:, q, n, :], ALU.add)\
                            .then_inc(na_biased.sem, 1)
                        dve.wait_ge(*na_biased(2 * n + q))
                        dve.tensor_reduce(na_max[:, n, q:q + 1], p[:, q, :], AX.X, ALU.max, negate=True)\
                            .then_inc(na_max_made.sem, 1)
                    else:
                        dve.wait_ge(*na_copied(part))
                        dve.tensor_reduce(na_max[:, n, :], p[:, :, 0:T], AX.X, ALU.max, negate=True)\
                            .then_inc(na_max_made.sem, 1)

            def na_normalise(n):
                p = na_probs[:, n % 3]
                cols = slice(0, T2 if n < H else T)
                dve.wait_ge(*na_exp(2 * n + 1))
                dve.reciprocal(na_recip[:, n, :], na_sum[:, n, :]).then_inc(na_recips.sem, 1)
                dve.wait_ge(*na_recips(n))
                for q in range(2):
                    dve.tensor_scalar(p[:, q, cols], p[:, q, cols], na_recip[:, n, q:q + 1], None, ALU.mult)\
                        .then_inc(na_probs_made.sem, 1)

            for i in range(2 * H):
                na_softmax(i)
                na_normalise(i)

            for t in range(WT):
                dve.wait_ge(*done2(f"mix{t}"))
                dve.wait_ge(*gelu_made(3))
                s = branches[:, WT + t, :]
                dve.tensor_tensor(s.rearrange("p (b q) -> p b q", b=4), bank2(f"mix{t}").rearrange("p (b q) -> p b q", b=4),
                                  sgu_b[:, t, :].unsqueeze(1).to_broadcast([P, 4, P]), ALU.add).then_inc(mix_biased.sem, 1)
                dve.wait_ge(*mix_biased(t))
                dve.tensor_tensor(s, s, sgu_in[:, t, :], ALU.mult).then_inc(mix_made.sem, 1)
            norm_out(0, 1)
            norm_in(2, 2)
            feed_forward2(0)
            norm_out(1, 3)

            dve.wait_ge(*y2_scaled(2 * KD - 1))
            layer_gains(1)
            norm_in(3, 0)
            dve.wait_ge(loaded["axial"], 32)
            for f in range(2 * H):
                name = f"ret_qk{f}"
                a, b = ret_t[:, 2 * (f % 4), :], ret_t[:, 2 * (f % 4) + 1, :]
                dve.wait_ge(*done2(name))
                if f >= 4:
                    dve.wait_ge(*rot_made(f - 4))
                if f >= H:
                    dve.wait_ge(*rot_ctx(f - H))
                dve.tensor_tensor(a, bank2(name)[:, 0:T], rope_c[:, :], ALU.mult)
                for to, of in ((slice(0, 64), slice(64, P)), (slice(64, P), slice(0, 64))):
                    r = dve.tensor_tensor(b[to, :], bank2(name)[of, 0:T], rope_s[of, :], ALU.mult)
                r.then_inc(rot_mul.sem, 1)
            for c in range(4):
                e, g = ret_e[:, 4 * c:4 * c + 4, :], ret_g[:, 4 * c:4 * c + 4, :]
                dve.wait_ge(*ret_g_one(c))
                dve.reciprocal(e, e).then_inc(ret_g_recip.sem, 1)
                dve.wait_ge(*ret_g_recip(c))
                dve.tensor_tensor(g, g, e, ALU.mult).then_inc(ret_silu.sem, 1)
            for i in range(H + 4):
                if i < H:
                    dve.wait_ge(*decay_made(i))
                    for b in range(2):
                        if i >= 2 and b == 0:
                            dve.wait_ge(*done2(f"ret_o{i - 2}"))
                        dve.wait_ge(*done2(f"ret_score{i}_{b}"))
                        dve.scalar_tensor_tensor(decayed[:, i % 2, 2 * b:2 * b + 2, :].rearrange("p a b -> p (a b)"),
                                                 bank2(f"ret_score{i}_{b}"), P ** -0.5,
                                                 decay[:, i % 2, 2 * b:2 * b + 2, :].rearrange("p a b -> p (a b)"),
                                                 ALU.mult, ALU.mult).then_inc(ret_decayed.sem, 1)
                if 0 <= i - 2 < H:
                    h = i - 2
                    o = ret_o[:, h % 3]
                    dve.wait_ge(*done2(f"ret_mean{h}"))
                    dve.tensor_tensor(o, o, bank2(f"ret_mean{h}")[:, 0:T].unsqueeze(1).to_broadcast([P, 2, T]), ALU.subtract)\
                        .then_inc(ret_centred.sem, 1)
                if 0 <= i - 4 < H:
                    h = i - 4
                    dve.wait_ge(*ret_root(h))
                    for half in range(2):
                        a = dve.scalar_tensor_tensor(ret_o[:, h % 3, half, :], ret_o[:, h % 3, half, :],
                                                     misc_of("gn_g")[:, 2 * h + half:2 * h + half + 1], ret_rstd[:, h % 2, :],
                                                     ALU.mult, ALU.mult)
                    a.then_inc(ret_normed.sem, 1)
            norm_out(2, 1)
            norm_in(4, 2)
            feed_forward2(1)
            norm_out(3, 3)

        @block.gpsimd
        def _(pool):
            pool.wait_ge(loaded["cst"], 16)
            with pool.Fori(0, DEPTH) as l:
                one = const("ones")[:, 0:1].to_broadcast([P, T])
                before = const("before").unsqueeze(1).to_broadcast([P, 2, P])

                def diagonals(t):
                    return t.rearrange("p (a b) -> p a b", b=P)[:, 0:3:2, :]

                def mask_keep(s):
                    h = s - 2 * H
                    pool.wait_ge(*keep_made(h, l))
                    d = diagonals(log_keep[:, s % 3, :])
                    pool.tensor_tensor(d, d, before, ALU.mult).then_inc(keep_masked.sem, 1)

                def mask_stick(s):
                    h = s - 2 * H
                    pool.wait_ge(*stick_exp(h, l))
                    d = diagonals(keys[:, s % 2, :])
                    pool.tensor_tensor(d, d, before, ALU.mult).then_inc(stick_made.sem, 1)

                for i in range(STEPS + 1):
                    if 2 * H <= i < STEPS:
                        mask_keep(i)
                    if i < STEPS:
                        pool.wait_ge(*gate_exp(i, l))
                        pool.tensor_tensor(sigma[:, i, :], sigma[:, i, :], one, ALU.add).then_inc(gate_one.sem, 1)
                    if 2 * H < i:
                        mask_stick(i - 1)
                for b in range(1, 3):
                    for f in range(KD):
                        n = (b - 1) * KD + f
                        pool.wait_ge(*gated_made(b * KD + f, l))
                        if b == 2:
                            pool.wait_ge(*merged_made(f, l))
                        pool.tensor_tensor(merged[:, f, :], merged[:, f, :], gated[:, n % 2, :], ALU.add)\
                            .then_inc(merged_made.sem, 1)
                for f in range(FT):
                    pool.wait_ge(*ffn_exp(f, l))
                    pool.tensor_tensor(ffn_e[:, f % 3, :], ffn_e[:, f % 3, :], one, ALU.add).then_inc(ffn_one.sem, 1)

            def add_residual(m):
                n = T2 if m < 2 else T
                for k in range(KD):
                    pool.wait_ge(*y2_scaled(m * KD + k))
                    pool.tensor_tensor(x[:, k, 0:n], x[:, k, 0:n], Y_OF[m][:, k, :], ALU.add).then_inc(x2_made.sem, 1)

            def feed_forward2(j):
                conv = wide_conv if j == 0 else thin_conv
                for f in range(FT):
                    e = conv[:, 2, f % 2, :]
                    pool.wait_ge(*conv_exp(j * FT + f))
                    pool.tensor_scalar(e, e, 1.0, None, ALU.add).then_inc(conv_one.sem, 1)

            pool.wait_ge(loaded["na"], 16 * 3)
            for q in range(2):
                b = na_bias[:, q].rearrange("p h (k c) -> p (h k) c", c=GRID)
                pool.tensor_tensor(b, b, const("na_mask").unsqueeze(1).to_broadcast([P, H * ROWS, GRID]), ALU.add)\
                    .then_inc(bias_masked.sem, 1)
            for c in range(4):
                t = sgu_t[:, c % 2, :]
                pool.wait_ge(*gelu_sq(c))
                pool.tensor_scalar(t, t, 0.044715, None, ALU.mult).then_inc(gelu_poly.sem, 1)
                pool.wait_ge(*gelu_poly(2 * c))
                pool.tensor_scalar(t, t, 1.0, None, ALU.add).then_inc(gelu_poly.sem, 1)
                pool.wait_ge(*gelu_exp(c))
                pool.tensor_scalar(t, t, 1.0, None, ALU.add).then_inc(gelu_one.sem, 1)
            add_residual(0)
            feed_forward2(0)
            add_residual(1)

            for f in range(2 * H):
                a, b = ret_t[:, 2 * (f % 4), :], ret_t[:, 2 * (f % 4) + 1, :]
                pool.wait_ge(*rot_mul(f))
                pool.tensor_tensor(ret_q[:, f, :] if f < H else ret_k[:, f - H, 0:T], a, b, ALU.add).then_inc(rot_made.sem, 1)

            def decays(h):
                fwd, bwd = decay[:, h % 2], decay_b
                for d, t in enumerate((fwd, bwd)):
                    pool.wait_ge(*decay_exp(2 * h + d))
                    pool.tensor_tensor(t[:, 0:2, :], t[:, 0:2, :], ret_mask[:, 2 * d:2 * d + 2, :], ALU.mult)\
                        .then_inc(decay_masked.sem, 1)
                pool.wait_ge(*decay_masked(2 * h + 1))
                pool.tensor_tensor(fwd, fwd, bwd, ALU.add).then_inc(decay_made.sem, 1)

            pool.wait_ge(loaded["mask"], 16)
            decays(0)
            for c in range(4):
                e = ret_e[:, 4 * c:4 * c + 4, :]
                pool.wait_ge(*ret_g_exp(c))
                pool.tensor_scalar(e, e, 1.0, None, ALU.add).then_inc(ret_g_one.sem, 1)
            for i in range(H + 4):
                if i + 1 < H:
                    decays(i + 1)
                if 0 <= i - 4 < H:
                    h = i - 4
                    pool.wait_ge(*ret_normed(h))
                    pool.wait_ge(*ret_silu(3))
                    g = ret_g[:, 2 * h:2 * h + 2, :]
                    pool.tensor_tensor(g, g, ret_o[:, h % 3], ALU.mult).then_inc(ret_gated.sem, 1)
            add_residual(2)
            feed_forward2(1)
            add_residual(3)


def kernel(**inputs):
    import concourse.bacc as bacc
    from concourse.bass_utils import run_bass_kernel_spmd

    i = {k: np.asarray(v) for k, v in inputs.items()}
    adas = [i["w_ada"][0], i["w_ada"][1], i["ada_w_2"][0], i["ada_w_2"][1]]
    parts = [panels([stationary(adas[0])])] + [tape_block1(i, l, adas[l + 1]) for l in range(DEPTH)]
    parts += [tape_block2(i, j, adas[3] if j == 0 else None) for j in range(2)]
    tape = np.concatenate(parts)
    pad = -len(tape) % RING
    tape = np.concatenate([tape, np.zeros((pad, P, PANEL), np.float32)])
    par1 = np.zeros((P, DEPTH, N_PAR1), np.float32)
    for l in range(DEPTH):
        for n, v in (("b_ada", i["b_ada"]), ("g_mix", i["g_mix"]), ("g_ffn", i["g_ffn"]), ("g_q", i["g_mla_q"]),
                     ("g_kv", i["g_mla_kv"])):
            a, w = PAR1[n]
            par1[:, l, a:a + w] = feature_major(v[l])
        par1[:H, l, PAR1["b_fox"][0]] = i["b_fox_f"][l]
    par2 = np.zeros((P, DEPTH, N_PAR2), np.float32)
    for j in range(DEPTH):
        for n, v in (("b_ada", i["ada_b_2"][j]), ("norm_g", i["norm_g_2"][j].reshape(-1)),
                     ("conv_w", i["ffn_conv_w_2"][j].reshape(-1)), ("conv_b", i["ffn_conv_b_2"][j])):
            a, w = PAR2[n]
            par2[:, j, a:a + w] = feature_major(v)
    misc = np.concatenate([feature_major(i["g_final"]), feature_major(i["ret_gn_g_2"][0]),
                           np.broadcast_to(i["ret_log_decay_2"][0].reshape(1, -1), (P, 2 * H))], 1)
    sgu_w = i["sgu_w_2"][0].transpose(2, 0, 1)
    sgu_b = np.repeat(i["sgu_b_2"][0].reshape(WT, 2, 1, P), DH, axis=2).reshape(WT, P, P).transpose(1, 0, 2)
    dist, mask = retention_constants()
    cond = np.stack([feature_major(i["c"][0]), feature_major(i["c_2"][0]), feature_major(i["c_ctx_2"])], 2)
    feed = {
        "tape": tape,
        "consts": np.concatenate(list(shape_constants().values()), 1),
        "par1": par1,
        "cond": np.ascontiguousarray(cond),
        "pos": i["positions"].reshape(T),
        "x_t": np.ascontiguousarray(i["x"][0].T.reshape(KD, P, T).transpose(1, 0, 2)),
        "par2": par2,
        "misc": np.ascontiguousarray(misc),
        "ctx": np.ascontiguousarray(i["ctx_2"][0].T.reshape(KD, P, T).transpose(1, 0, 2)),
        "bias": bias_window(i["na_rpb_2"][0]),
        "sgu_w": np.ascontiguousarray(sgu_w),
        "sgu_b": np.ascontiguousarray(sgu_b),
        "axial": axial_rope(),
        "dist": dist,
        "mask": mask,
    }
    nc = bacc.Bacc("TRN2", target_bir_lowering=False, num_devices=1)
    args = [nc.dram_tensor(n + "_in", a.shape, mybir.dt.from_np(a.dtype), kind="ExternalInput").ap() for n, a in feed.items()]
    out = nc.dram_tensor("out_t", (P, KD, T), F32, kind="ExternalOutput").ap()
    two_blocks(nc, *args, out)
    r = run_bass_kernel_spmd(nc, [{n + "_in": a for n, a in feed.items()}], core_ids=[0])
    got = r.results[0]["out_t"]
    return np.ascontiguousarray(got.transpose(2, 1, 0).reshape(1, T, D))
```
